# Optimizing a Trainium2 kernel written in Bass

```python
import functools
import jax
import jax.numpy as jnp
from jax import lax
import numpy as np

D_MODEL = 1024
BATCH = 1
SEQ = 256
DEPTH = 2
DEC_BATCH = 8
DEC_SEQ = 8
PAST_LEN = 2048
PAGE_SIZE = 128

HEAD_DIM = 64
N_HEADS_A = 8
N_HEADS_B = 8
W_A = N_HEADS_A * HEAD_DIM
W_B = N_HEADS_B * HEAD_DIM
DILATED_PATTERNS = ((128, 1), (512, 4), (2048, 16))
WIN_MAX = 2048
MOBA_BLOCK = 256
MOBA_TOPK = 3
MOBA_QCHUNK = 16
N_HEADS_C = 8
HEAD_DIM_C = 64
W_C = N_HEADS_C * HEAD_DIM_C
DECAY_RANK = 64
ICLR_RANK = 64
GATE_RANK = 160
C_COLS = 3 * W_C + DECAY_RANK + ICLR_RANK + GATE_RANK
N_HEADS_D = 4
HEAD_DIM_D = 128
W_D = N_HEADS_D * HEAD_DIM_D
RET_CHUNK = 128
D_FF = 2816
N_EXPERTS = 8
TOP_K = 2
MOE_BLOCK = 128
RMS_EPS = 1e-6
GN_EPS = 64e-5
NEG = -1e30
F32 = jnp.float32

kernel_name = 'hybrid_dilated_moba_rwkv7_retention_step'

def rmsnorm(x, g):
    xf = x.astype(F32)
    y = xf * lax.rsqrt(jnp.mean(xf * xf, axis=-1, keepdims=True) + RMS_EPS)
    return (y * g.astype(F32)).astype(x.dtype)

def heads(t, n):
    return t.reshape(t.shape[:-1] + (n, t.shape[-1] // n))

def softmax_stats(s, valid):
    s = jnp.where(valid, s, NEG)
    m = jnp.max(s, axis=-1, keepdims=True)
    e = jnp.where(valid, jnp.exp(s - m), 0.0)
    l = jnp.maximum(jnp.sum(e, axis=-1, keepdims=True), 1e-30)
    return e / l, (m + jnp.log(l))[..., 0]

def merge_by_denominator(parts):
    lse = functools.reduce(jnp.logaddexp, [l for _, l in parts])
    return sum(o * jnp.exp(l - lse)[..., None] for o, l in parts)

def swiglu(x, w1, w3, w2):
    return jnp.dot(jax.nn.silu(jnp.dot(x, w1)) * jnp.dot(x, w3), w2)

def dilated_prompt(q, k, v):
    B, S, H, hd = q.shape
    scale = hd ** -0.5
    parts = []
    for window, dil in DILATED_PATTERNS:
        nk = window // dil
        L = S // dil
        nb = -(-L // nk)

        def strided_blocks(t):
            t = t.reshape(B, L, dil, H, hd).transpose(0, 2, 3, 1, 4)
            t = jnp.pad(t, ((0, 0), (0, 0), (0, 0), (0, nb * nk - L), (0, 0)))
            return t.reshape(B, dil, H, nb, nk, hd)

        def with_previous(t):
            prev = jnp.pad(t, ((0, 0),) * 3 + ((1, 0), (0, 0), (0, 0)))[:, :, :, :-1]
            return jnp.concatenate([prev, t], axis=4)

        qb = strided_blocks(q)
        kb = with_previous(strided_blocks(k))
        vb = with_previous(strided_blocks(v))
        s = jnp.einsum('brhnqe,brhnke->brhnqk', qb, kb, preferred_element_type=F32) * scale
        qi = jnp.arange(nk)[:, None]
        ki = jnp.arange(2 * nk)[None, :]
        steps = nk + qi - ki
        valid = (steps >= 0) & (steps <= nk) & ((jnp.arange(nb)[:, None, None] > 0) | (ki >= nk))
        p, lse = softmax_stats(s, valid)
        o = jnp.einsum('brhnqk,brhnke->brhnqe', p, vb.astype(F32))
        o = o.reshape(B, dil, H, nb * nk, hd)[:, :, :, :L].transpose(0, 3, 1, 2, 4).reshape(B, S, H, hd)
        lse = lse.reshape(B, dil, H, nb * nk)[..., :L].transpose(0, 3, 1, 2).reshape(B, S, H)
        parts.append((o, lse))
    return merge_by_denominator(parts)

def dilated_sample(q, k_all, v_all, n_buf):
    T = q.shape[1]
    scale = q.shape[-1] ** -0.5
    parts = []
    for window, dil in DILATED_PATTERNS:
        nk = window // dil
        idx = n_buf + jnp.arange(T)[:, None] - dil * jnp.arange(nk + 1)[None, :]
        valid = (idx >= 0)[None, :, None, :]
        idx = jnp.maximum(idx, 0)
        kg, vg = k_all[:, idx], v_all[:, idx]
        s = jnp.einsum('bthe,btjhe->bthj', q, kg, preferred_element_type=F32) * scale
        p, lse = softmax_stats(s, valid)
        o = jnp.einsum('bthj,btjhe->bthe', p, vg.astype(F32))
        parts.append((o, lse))
    return merge_by_denominator(parts)

def moba_select(gate, q_block):
    nbk = gate.shape[-1]
    full_past = jnp.arange(nbk)[None, None, :] < q_block[:, None, None]
    g = jnp.where(full_past, gate, NEG)
    if nbk < MOBA_TOPK:
        g = jnp.pad(g, [(0, 0)] * (g.ndim - 1) + [(0, MOBA_TOPK - nbk)], constant_values=NEG)
    vals, idx = lax.top_k(g, MOBA_TOPK)
    return jnp.clip(idx, 0, max(nbk - 1, 0)), vals > 0.5 * NEG

def moba_prompt(q, k, v):
    B, S, H, hd = q.shape
    scale = hd ** -0.5
    nb = -(-S // MOBA_BLOCK)
    pad = ((0, 0), (0, nb * MOBA_BLOCK - S), (0, 0), (0, 0))
    qb, kb, vb = [jnp.pad(t, pad).reshape(B, nb, MOBA_BLOCK, H, hd) for t in (q, k, v)]
    s = jnp.einsum('bnqhe,bnkhe->bnhqk', qb, kb, preferred_element_type=F32) * scale
    p, lse_own = softmax_stats(s, jnp.tril(jnp.ones((MOBA_BLOCK, MOBA_BLOCK), bool)))
    o_own = jnp.einsum('bnhqk,bnkhe->bnqhe', p, vb.astype(F32)).reshape(B, nb * MOBA_BLOCK, H, hd)[:, :S]
    lse_own = lse_own.transpose(0, 1, 3, 2).reshape(B, nb * MOBA_BLOCK, H)[:, :S]
    k_mean = jnp.mean(kb.astype(F32), axis=2)
    gate = jnp.einsum('bshe,bnhe->bshn', q.astype(F32), k_mean)
    sel, sel_valid = moba_select(gate, jnp.arange(S) // MOBA_BLOCK)
    nq = S // MOBA_QCHUNK

    def to_chunks(t):
        return t.reshape((B, nq, MOBA_QCHUNK) + t.shape[2:]).swapaxes(0, 1)

    bi = jnp.arange(B)[:, None, None, None]
    hi = jnp.arange(H)[None, None, :, None]
    n_sel = MOBA_TOPK * MOBA_BLOCK

    def attend_selected(args):
        qc, sc, vc = args
        kg = kb[bi, sc, :, hi].reshape(B, MOBA_QCHUNK, H, n_sel, hd)
        vg = vb[bi, sc, :, hi].reshape(B, MOBA_QCHUNK, H, n_sel, hd)
        s_c = jnp.einsum('bqhe,bqhne->bqhn', qc, kg, preferred_element_type=F32) * scale
        p_c, lse_c = softmax_stats(s_c, jnp.repeat(vc, MOBA_BLOCK, axis=-1))
        return jnp.einsum('bqhn,bqhne->bqhe', p_c, vg.astype(F32)), lse_c

    o_sel, lse_sel = lax.map(attend_selected, (to_chunks(q), to_chunks(sel), to_chunks(sel_valid)))
    o_sel = o_sel.swapaxes(0, 1).reshape(B, S, H, hd)
    lse_sel = lse_sel.swapaxes(0, 1).reshape(B, S, H)
    return merge_by_denominator([(o_own, lse_own), (o_sel, lse_sel)])

def moba_sample(q, k_new, v_new, pool, page_table):
    Bd, T, H, hd = q.shape
    scale = hd ** -0.5
    n_pages = page_table.shape[1]
    ps = pool.shape[1]
    past = n_pages * ps
    ppb = MOBA_BLOCK // ps
    nbp = past // MOBA_BLOCK
    qpos = past + jnp.arange(T)
    page_sums = jnp.sum(pool[:, :, 0].astype(F32), axis=1)
    k_mean = page_sums[page_table[:, :nbp * ppb]].reshape(Bd, nbp, ppb, H, hd).sum(axis=2) / MOBA_BLOCK
    gate = jnp.einsum('bthe,bnhe->bthn', q.astype(F32), k_mean)
    sel, sel_valid = moba_select(gate, qpos // MOBA_BLOCK)
    lpage = jnp.clip(sel[..., None] * ppb + jnp.arange(ppb), 0, n_pages - 1)
    phys = page_table[jnp.arange(Bd)[:, None, None, None, None], lpage]
    kv_sel = pool[phys, :, :, jnp.arange(H)[None, None, :, None, None]]
    kv_sel = kv_sel.reshape(Bd, T, H, MOBA_TOPK * MOBA_BLOCK, 2, hd)
    b0 = (past // MOBA_BLOCK) * MOBA_BLOCK
    kv_own = pool[page_table[:, b0 // ps:]].reshape(Bd, past - b0, 2, H, hd)
    k_own = jnp.concatenate([kv_own[:, :, 0].astype(k_new.dtype), k_new], axis=1)
    v_own = jnp.concatenate([kv_own[:, :, 1].astype(v_new.dtype), v_new], axis=1)
    s_sel = jnp.einsum('bthe,bthne->bthn', q, kv_sel[..., 0, :], preferred_element_type=F32) * scale
    s_own = jnp.einsum('bthe,bkhe->bthk', q, k_own, preferred_element_type=F32) * scale
    own_pos = b0 + jnp.arange(k_own.shape[1])
    valid = jnp.concatenate([
        jnp.broadcast_to(jnp.repeat(sel_valid, MOBA_BLOCK, axis=-1), s_sel.shape),
        jnp.broadcast_to((own_pos[None, :] <= qpos[:, None])[None, :, None, :], s_own.shape)], axis=-1)
    p, _ = softmax_stats(jnp.concatenate([s_sel, s_own], axis=-1), valid)
    n_sel = s_sel.shape[-1]
    return (jnp.einsum('bthn,bthne->bthe', p[..., :n_sel], kv_sel[..., 1, :].astype(F32))
            + jnp.einsum('bthk,bkhe->bthe', p[..., n_sel:], v_own.astype(F32)))

def rwkv7_scan(r, w, k, v, kk, a, s0):
    def step(s, inp):
        r_t, w_t, k_t, v_t, kk_t, a_t = inp
        sa = jnp.einsum('bhvk,bhk->bhv', s, -kk_t)
        s = (s * w_t[:, :, None, :] + sa[..., None] * (kk_t * a_t)[:, :, None, :]
             + v_t[..., None] * k_t[:, :, None, :])
        return s, jnp.einsum('bhvk,bhk->bhv', s, r_t)

    s, y = lax.scan(step, s0, tuple(t.swapaxes(0, 1) for t in (r, w, k, v, kk, a)))
    return y.swapaxes(0, 1), s

def rotate_retention(x, pos):
    hd = x.shape[-1]
    angle = 1.0 / (10000.0 ** jnp.linspace(0.0, 1.0, hd // 2, dtype=F32))
    theta = pos[:, None] * jnp.repeat(angle, 2)[None, :]
    sin = jnp.sin(theta)[None, :, None, :]
    cos = jnp.cos(theta)[None, :, None, :]
    rot = jnp.stack([-x[..., 1::2], x[..., ::2]], axis=-1).reshape(x.shape)
    return x * cos + rot * sin

def retention_chunkwise(q, k, v, r0):
    B, T, H, hd = q.shape
    C = min(RET_CHUNK, T)
    n = T // C
    log_g = jnp.log1p(-jnp.power(2.0, -5.0 - jnp.arange(H, dtype=F32)))
    i = jnp.arange(C, dtype=F32)
    diff = i[:, None] - i[None, :]
    dmask = jnp.where(diff >= 0, jnp.exp(jnp.maximum(diff, 0.0)[None] * log_g[:, None, None]), 0.0)
    q_dec = jnp.exp((i[:, None] + 1.0) * log_g[None, :])
    k_dec = jnp.exp((C - 1.0 - i)[:, None] * log_g[None, :])
    chunk_dec = jnp.exp(C * log_g)

    def step(R, inp):
        qc, kc, vc = inp
        s = jnp.einsum('bqhe,bkhe->bhqk', qc, kc) * dmask
        o = (jnp.einsum('bhqk,bkhe->bqhe', s, vc)
             + jnp.einsum('bqhe,bhef->bqhf', qc, R) * q_dec[None, :, :, None])
        R = R * chunk_dec[None, :, None, None] + jnp.einsum('bkhe,bkhf->bhef', kc * k_dec[None, :, :, None], vc)
        return R, o

    xs = tuple(t.reshape(B, n, C, H, hd).swapaxes(0, 1) for t in (q, k, v))
    R, o = lax.scan(step, r0, xs)
    return o.swapaxes(0, 1).reshape(B, T, H, hd), R

def odd_mixer(h, shift_prev, s_rwkv, r_ret, pos0, w_in, w_out, mu_shift, w0, w_up, a0, a_up, g_up,
              k_k, k_a, r_k, lnx_w, lnx_b):
    B, T, _ = h.shape
    proj = jnp.dot(h, w_in)
    pc, pd = proj[..., :C_COLS], proj[..., C_COLS:]
    prev = jnp.concatenate([shift_prev[:, None, :].astype(pc.dtype), pc[:, :-1]], axis=1)
    xm = (pc + (prev - pc) * mu_shift).astype(F32)
    o1, o2, o3 = W_C, 2 * W_C, 3 * W_C
    o4, o5 = o3 + DECAY_RANK, o3 + DECAY_RANK + ICLR_RANK
    r, k, v = xm[..., :o1], xm[..., o1:o2], xm[..., o2:o3]
    wd, ad, gd = xm[..., o3:o4], xm[..., o4:o5], xm[..., o5:]
    log_w = -jax.nn.softplus(-(w0 + jnp.dot(jnp.tanh(wd), w_up))) - 0.5
    decay = jnp.exp(-jnp.exp(log_w))
    a = jax.nn.sigmoid(a0 + jnp.dot(ad, a_up))
    g = jnp.dot(jax.nn.sigmoid(gd), g_up)
    kk = heads(k * k_k, N_HEADS_C)
    kk = kk / jnp.maximum(jnp.linalg.norm(kk, axis=-1, keepdims=True), 1e-12)
    k = k * (1.0 + (a - 1.0) * k_a)
    rh, kh, vh, wh, ah = (heads(t, N_HEADS_C) for t in (r, k, v, decay, a))
    y, s_new = rwkv7_scan(rh, wh, kh, vh, kk, ah, s_rwkv.astype(F32))
    mu = jnp.mean(y, axis=-1, keepdims=True)
    var = jnp.mean(jnp.square(y - mu), axis=-1, keepdims=True)
    y = ((y - mu) * lax.rsqrt(var + GN_EPS)).reshape(B, T, W_C) * lnx_w + lnx_b
    y = y + (jnp.sum(rh * kh * r_k, axis=-1, keepdims=True) * vh).reshape(B, T, W_C)
    y_c = y * g
    pdf = pd.astype(F32)
    qd = heads(pdf[..., :W_D], N_HEADS_D)
    kd = heads(pdf[..., W_D:2 * W_D], N_HEADS_D)
    vd = heads(pdf[..., 2 * W_D:3 * W_D], N_HEADS_D)
    gate_d = pdf[..., 3 * W_D:]
    pos = (pos0 + jnp.arange(T)).astype(F32)
    qd = rotate_retention(qd, pos)
    kd = rotate_retention(kd, pos) * HEAD_DIM_D ** -0.5
    o, r_new = retention_chunkwise(qd, kd, vd, r_ret.astype(F32))
    o = o * lax.rsqrt(jnp.mean(o * o, axis=-1, keepdims=True) + RMS_EPS)
    y_d = o.reshape(B, T, W_D) * jax.nn.silu(gate_d)
    out = jnp.dot(jnp.concatenate([y_c, y_d], axis=-1).astype(h.dtype), w_out)
    return out, (s_new.astype(s_rwkv.dtype), pc[:, -1], r_new.astype(r_ret.dtype))

def moe_swiglu(h, router_w, w1, w3, w2):
    shape = h.shape
    xt = h.reshape(-1, shape[-1])
    n = xt.shape[0]
    logits = jnp.dot(xt.astype(F32), router_w.astype(F32))
    top_logit, top_e = lax.top_k(logits, TOP_K)
    gates = jax.nn.softmax(top_logit, axis=-1).reshape(-1)
    flat_e = top_e.reshape(-1)
    flat_tok = jnp.repeat(jnp.arange(n, dtype=jnp.int32), TOP_K)
    order = jnp.argsort(flat_e)
    e_sorted = flat_e[order]
    counts = jnp.bincount(flat_e, length=N_EXPERTS)
    padded = (counts + MOE_BLOCK - 1) // MOE_BLOCK * MOE_BLOCK
    pad_end = jnp.cumsum(padded)
    pad_start = pad_end - padded
    grp_start = jnp.cumsum(counts) - counts
    dest = pad_start[e_sorted] + jnp.arange(n * TOP_K) - grp_start[e_sorted]
    n_blocks = -(-(n * TOP_K + N_EXPERTS * (MOE_BLOCK - 1)) // MOE_BLOCK)
    cap = n_blocks * MOE_BLOCK
    slot_tok = jnp.full((cap,), n, jnp.int32).at[dest].set(flat_tok[order])
    slot_gate = jnp.zeros((cap,), F32).at[dest].set(gates[order])
    block_e = jnp.minimum(jnp.searchsorted(pad_end, jnp.arange(n_blocks) * MOE_BLOCK, side='right'),
                          N_EXPERTS - 1)
    x_slots = jnp.concatenate([xt, jnp.zeros((1, shape[-1]), xt.dtype)], axis=0)[slot_tok]
    y = lax.map(lambda a: swiglu(a[0], w1[a[1]], w3[a[1]], w2[a[1]]),
                (x_slots.reshape(n_blocks, MOE_BLOCK, shape[-1]), block_e))
    out = jax.ops.segment_sum(y.reshape(cap, shape[-1]).astype(F32) * slot_gate[:, None], slot_tok,
                              num_segments=n + 1)[:n]
    return out.astype(h.dtype).reshape(shape)

def trunk(x, c, mixers, ffns, norm_g, ada_w, ada_b, final_g):
    new_state = []
    for layer in range(DEPTH):
        mod = jnp.dot(jax.nn.silu(c), ada_w[layer]) + ada_b[layer]
        sh1, sc1, g1, sh2, sc2, g2 = jnp.split(mod[:, None, :], 6, axis=-1)
        out, st = mixers[layer % 2](rmsnorm(x, norm_g[layer, 0]) * (1.0 + sc1) + sh1)
        x = x + g1 * out
        x = x + g2 * ffns[layer % 2](rmsnorm(x, norm_g[layer, 1]) * (1.0 + sc2) + sh2)
        new_state.extend(st)
    return rmsnorm(x, final_g), new_state

def setup_inputs(seed: int = 0) -> dict:
    key = jax.random.key(seed)
    ks = iter(jax.random.split(key, 48))

    def nrm(shape, s=1.0):
        return jax.random.normal(next(ks), shape, F32) * s

    n_pages = PAST_LEN // PAGE_SIZE
    n_pool = (DEC_BATCH * n_pages * 5) // 4
    win_buf = min(WIN_MAX, PAST_LEN)
    page_table = jax.random.permutation(next(ks), n_pool)[:DEC_BATCH * n_pages].reshape(
        DEC_BATCH, n_pages).astype(jnp.int32)
    return {
        'x_prompt': nrm((BATCH, SEQ, D_MODEL)),
        'x_sample': nrm((DEC_BATCH, DEC_SEQ, D_MODEL)),
        'cache_win_kv': nrm((DEC_BATCH, win_buf, 2, N_HEADS_A, HEAD_DIM)),
        'cache_moba_kv': nrm((n_pool, PAGE_SIZE, 2, N_HEADS_B, HEAD_DIM)),
        'state_rwkv': nrm((DEC_BATCH, N_HEADS_C, HEAD_DIM_C, HEAD_DIM_C), 0.3),
        'state_shift': nrm((DEC_BATCH, C_COLS)),
        'state_ret': nrm((DEC_BATCH, N_HEADS_D, HEAD_DIM_D, HEAD_DIM_D)),
        'page_table': page_table,
        'c_prompt': nrm((BATCH, D_MODEL)),
        'c_sample': nrm((DEC_BATCH, D_MODEL)),
        'norm_g': 1.0 + nrm((DEPTH, 2, D_MODEL), 0.02),
        'ada_w': nrm((DEPTH, D_MODEL, 6 * D_MODEL), 0.5 * D_MODEL ** -0.5),
        'ada_b': nrm((DEPTH, 6 * D_MODEL), 0.02),
        'final_g': 1.0 + nrm((D_MODEL,), 0.02),
        'w_in_even': nrm((D_MODEL, 3 * W_A + 3 * W_B), D_MODEL ** -0.5),
        'w_out_even': nrm((W_A + W_B, D_MODEL), (W_A + W_B) ** -0.5),
        'w_in_odd': nrm((D_MODEL, C_COLS + 4 * W_D), D_MODEL ** -0.5),
        'w_out_odd': nrm((W_C + W_D, D_MODEL), (W_C + W_D) ** -0.5),
        'mu_shift': jax.random.uniform(next(ks), (C_COLS,), F32),
        'w0': jax.random.uniform(next(ks), (W_C,), F32, -5.0, 0.0),
        'w_up': nrm((DECAY_RANK, W_C), 0.1),
        'a0': nrm((W_C,), 0.1),
        'a_up': nrm((ICLR_RANK, W_C), ICLR_RANK ** -0.5),
        'g_up': nrm((GATE_RANK, W_C), GATE_RANK ** -0.5),
        'k_k': 0.85 + nrm((W_C,), 0.05),
        'k_a': 1.0 + nrm((W_C,), 0.05),
        'r_k': nrm((N_HEADS_C, HEAD_DIM_C), 0.1),
        'lnx_w': 1.0 + nrm((W_C,), 0.02),
        'lnx_b': nrm((W_C,), 0.02),
        'ffn_w1': nrm((D_MODEL, D_FF), D_MODEL ** -0.5),
        'ffn_w3': nrm((D_MODEL, D_FF), D_MODEL ** -0.5),
        'ffn_w2': nrm((D_FF, D_MODEL), D_FF ** -0.5),
        'router_w': nrm((D_MODEL, N_EXPERTS), D_MODEL ** -0.5),
        'moe_w1': nrm((N_EXPERTS, D_MODEL, D_FF), D_MODEL ** -0.5),
        'moe_w3': nrm((N_EXPERTS, D_MODEL, D_FF), D_MODEL ** -0.5),
        'moe_w2': nrm((N_EXPERTS, D_FF, D_MODEL), D_FF ** -0.5),
    }

def reference(x_prompt, x_sample, cache_win_kv, cache_moba_kv, state_rwkv, state_shift, state_ret, page_table,
              c_prompt, c_sample, norm_g, ada_w, ada_b, final_g, w_in_even, w_out_even, w_in_odd, w_out_odd,
              mu_shift, w0, w_up, a0, a_up, g_up, k_k, k_a, r_k, lnx_w, lnx_b, ffn_w1, ffn_w3, ffn_w2,
              router_w, moe_w1, moe_w3, moe_w2):
    past_len = page_table.shape[1] * cache_moba_kv.shape[1]
    odd_w = (w_in_odd, w_out_odd, mu_shift, w0, w_up, a0, a_up, g_up, k_k, k_a, r_k, lnx_w, lnx_b)

    def even_project(h):
        p = jnp.dot(h, w_in_even)
        qa, ka, va = (heads(p[..., i * W_A:(i + 1) * W_A], N_HEADS_A) for i in range(3))
        qb, kb, vb = (heads(p[..., 3 * W_A + i * W_B:3 * W_A + (i + 1) * W_B], N_HEADS_B) for i in range(3))
        return qa, ka, va, qb, kb, vb

    def even_output(o_a, o_b, h):
        B, T = h.shape[:2]
        o = jnp.concatenate([o_a.reshape(B, T, W_A), o_b.reshape(B, T, W_B)], axis=-1).astype(h.dtype)
        return jnp.dot(o, w_out_even)

    def even_prompt(h):
        S = h.shape[1]
        qa, ka, va, qb, kb, vb = even_project(h)
        out = even_output(dilated_prompt(qa, ka, va), moba_prompt(qb, kb, vb), h)
        n_keep = min(WIN_MAX, S)
        return out, (jnp.stack([ka, va], axis=2)[:, S - n_keep:], jnp.stack([kb, vb], axis=2))

    def even_sample(h):
        qa, ka, va, qb, kb, vb = even_project(h)
        buf = cache_win_kv.astype(ka.dtype)
        k_all = jnp.concatenate([buf[:, :, 0], ka], axis=1)
        v_all = jnp.concatenate([buf[:, :, 1], va], axis=1)
        out = even_output(dilated_sample(qa, k_all, v_all, buf.shape[1]),
                          moba_sample(qb, kb, vb, cache_moba_kv, page_table), h)
        return out, (jnp.stack([ka, va], axis=2), jnp.stack([kb, vb], axis=2))

    def odd_prompt(h):
        B = h.shape[0]
        return odd_mixer(h, jnp.zeros((B, C_COLS), h.dtype),
                         jnp.zeros((B, N_HEADS_C, HEAD_DIM_C, HEAD_DIM_C), h.dtype),
                         jnp.zeros((B, N_HEADS_D, HEAD_DIM_D, HEAD_DIM_D), h.dtype), 0, *odd_w)

    def odd_sample(h):
        return odd_mixer(h, state_shift, state_rwkv, state_ret, past_len, *odd_w)

    def dense_ffn(h):
        return swiglu(h, ffn_w1, ffn_w3, ffn_w2)

    def moe_ffn(h):
        return moe_swiglu(h, router_w, moe_w1, moe_w3, moe_w2)

    y_prompt, st_p = trunk(x_prompt, c_prompt, (even_prompt, odd_prompt), (dense_ffn, moe_ffn),
                           norm_g, ada_w, ada_b, final_g)
    y_sample, st_s = trunk(x_sample, c_sample, (even_sample, odd_sample), (dense_ffn, moe_ffn),
                           norm_g, ada_w, ada_b, final_g)
    win_p, moba_p, rwkv_p, shift_p, ret_p = st_p
    win_s, moba_s, rwkv_s, shift_s, ret_s = st_s
    return (y_prompt, y_sample, win_p, win_s, moba_p, moba_s, rwkv_p, rwkv_s, shift_p, shift_s, ret_p, ret_s)


_drawn_inputs = setup_inputs


def setup_inputs(seed=0):
    import zlib

    import numpy as np

    out = dict(_drawn_inputs(seed))
    spreads = {}
    factors = {'cache_moba_kv': 2.941, 'final_g': 2.736, 'lnx_w': 8.0, 'lnx_b': 8.0}
    for name, (base, spread) in spreads.items():
        noise = np.random.default_rng([zlib.crc32(name.encode()), seed]).standard_normal(out[name].shape)
        drawn = base * np.exp(spread * noise) if base else spread * noise
        out[name] = jnp.asarray(drawn.astype(out[name].dtype))
    for name, factor in factors.items():
        out[name] = (out[name] * factor).astype(out[name].dtype)
    return out
```

```python
from contextlib import ExitStack

import numpy as np
import concourse.bass as bass
from concourse import mybir

F32 = mybir.dt.float32
I32 = mybir.dt.int32
ALU = mybir.AluOpType
ACT = mybir.ActivationFunctionType
AX = mybir.AxisListType

P = 128
D = 1024
KT = D // P
SEQ = 256
NB, DT = 8, 8
NS = NB * DT
TOK = SEQ + NS
NC_ = 1 + NB
PAST, PAGE = 2048, 128
NPAGE = PAST // PAGE
NPOOL = NB * NPAGE * 5 // 4
NH, HD = 8, 64
W_MIX = NH * HD
C_COLS = 3 * W_MIX + 64 + 64 + 160
NHD, HDD = 4, 128
DFF = 2816
FT = DFF // P
NE = 8
MORE = (2 * TOK - 1) // P
CH = 32
NCH = SEQ // CH + NB
EPS, GN_EPS, NEG = 1e-6, 64e-5, -1e30
SCALE = HD ** -0.5
LOG_DECAY = -float(np.exp(-0.5))

VROWS = [("norm_g", 32), ("final_g", 8), ("mu_shift", 15), ("w0", 4), ("a0", 4), ("k_k", 4), ("k_a", 4),
         ("r_k", 4), ("lnx_w", 4), ("lnx_b", 4)]
VOFF, _n = {}, 0
for _name, _rows in VROWS:
    VOFF[_name] = _n
    _n += _rows
NV = _n
NADA = 2 * 6 * KT

FAR_TILES, NEAR_TILES = 6, 4
TILES_A, TILES_B = FAR_TILES + NEAR_TILES, NPAGE
NKA, NKB = TILES_A * P, TILES_B * P
CHUNKS_A, CHUNKS_B = (4, 4, 2), (4, 4, 4, 4)
SLOTS = 7


class Chain:

    def __init__(self, eng, sem):
        self.eng, self.sem, self.n, self.off = eng, sem, 0, 0

    def link(self, ins):
        self.n += 1
        ins.then_inc(self.sem, 1)
        self.eng.wait_ge(self.sem, self.n + self.off)

    def enter(self, i, per, ahead=0):
        self.base, self.per, self.off = self.n, per, i * per + ahead

    def leave(self, times):
        assert self.n - self.base == self.per, (self.n - self.base, self.per)
        self.n, self.off = self.base + self.per * times, 0


def hybrid_step(nc, io, stop=None):
    root = ExitStack()
    stage = [root]

    def sb(name, shape, dt=F32):
        return stage[-1].enter_context(nc.sbuf_tensor(name, shape, dt))

    sems = []

    def sem(name):
        sems.append(nc.alloc_semaphore(name=name))
        return sems[-1]

    names = [0]

    def uniq(name):
        names[0] += 1
        return f"{name}_{names[0]}"

    PS = root.enter_context(nc.psum_tensor("PS", [P, 8, 512], F32))
    X = sb("X", [P, KT, TOK])
    H = sb("H", [P, KT, TOK])
    MOD = sb("MOD", [P, 2, 6 * KT, NC_])
    GS = sb("GS", [P, 4, KT, NC_])
    VT = sb("VT", [P, NV])
    ident = sb("ident", [P, P])
    ones = sb("ones", [P, P])

    def setup_phase():
        XN = sb("XN", [P, 3, D])
        VN = sb("VN", [NV, P])
        AN = sb("AN", [NADA, P])
        CN = sb("CN", [NC_, D])
        CS = sb("CS", [NC_, D])
        ADAT = sb("ADAT", [P, NADA])
        CT = sb("CT", [P, KT, 32])
        R = 4
        RING = sb("ada_ring", [P, R, KT, 512])
        MN = sb("MN", [P, 2, 512])
        MS = sb("MS", [P, 2, 4, NC_])
        loaded_x, loaded_v, panel_in = sem("loaded_x"), sem("loaded_v"), [sem(f"ada_in{i}") for i in range(R)]
        ones_set, x_turned, x_copied, c_silu = sem("ones_set"), sem("x_turned"), sem("x_copied"), sem("c_silu")
        v_turned, v_copied, mod_done, mod_out, mod_turned, mod_set = (sem("v_turned"), sem("v_copied"), sem("mod_done"), sem("mod_out"),
                                                                      sem("mod_turned"), sem("mod_set"))
        gs_chain = sem("gs_chain")
        NPAN = 2 * 6 * D // 512

        with nc.Block() as block:
            @block.sync
            def _(sp):
                sp.dma_start(ident[:], io["ident"]).then_inc(loaded_x, 16)
                sp.dma_start(XN[:, 0:2, :], io["x_prompt"].rearrange("o (t p) d -> p (o t) d", p=P)).then_inc(loaded_x, 16)
                sp.dma_start(XN[0:NS, 2, :], io["x_sample"].rearrange("b t d -> (b t) d")).then_inc(loaded_x, 16)
                w = io["ada_w"].rearrange("l (k p) (j n) -> l j p k n", p=P, n=512)
                for n in range(NPAN):
                    if n >= R:
                        sp.wait_ge(mod_done, n - R + 1)
                    sp.dma_start(RING[:, n % R], w[n // 12, n % 12]).then_inc(panel_in[n % R], 16)

            @block.scalar
            def _(act):
                act.dma_start(VN[:], io["vectors"]).then_inc(loaded_v, 16)
                act.dma_start(AN[:], io["ada_b"].rearrange("l (r p) -> (l r) p", p=P)).then_inc(loaded_v, 16)
                act.dma_start(CN[0:1, :], io["c_prompt"]).then_inc(loaded_v, 16)
                act.dma_start(CN[1:NC_, :], io["c_sample"]).then_inc(loaded_v, 16)
                act.wait_ge(loaded_v, 64)
                nc.scalar.activation(CS[:], CN[:], ACT.Silu).then_inc(c_silu, 1)
                for n in range(NPAN):
                    act.wait_ge(mod_done, n + 1)
                    if n >= 2:
                        act.wait_ge(mod_turned, n - 1)
                    act.activation(MN[:, n % 2, :], PS[:, 4 + n % 2, :], ACT.Copy).then_inc(mod_out, 1)

            @block.gpsimd
            def _(gp):
                gp.memset(ones[:], 1.0).then_inc(ones_set, 1)
                gp.memset(CT[:], 0.0).then_inc(ones_set, 1)

            @block.tensor
            def _(pe):
                pe.wait_ge(loaded_x, 48)
                for k in range(KT):
                    for t, n in ((0, P), (1, P), (2, NS)):
                        last = pe.transpose(PS[:, k, t * P:t * P + n], XN[0:n, t, k * P:(k + 1) * P], ident[0:n, 0:n])
                    last.then_inc(x_turned, 1)
                pe.wait_ge(x_copied, KT)
                pe.wait_ge(c_silu, 1)
                pe.transpose(PS[:, 0, 0:NV], VN[:], ident[0:NV, 0:NV])
                pe.transpose(PS[:, 1, 0:NADA], AN[:], ident[0:NADA, 0:NADA])
                for k in range(KT):
                    last = pe.transpose(PS[:, 2, k * NC_:(k + 1) * NC_], CS[:, k * P:(k + 1) * P], ident[0:NC_, 0:NC_])
                last.then_inc(v_turned, 1)
                pe.wait_ge(v_copied, 3)

                def turn(n):
                    pe.wait_ge(mod_out, n + 1)
                    if n >= 2:
                        pe.wait_ge(mod_set, n - 1)
                    for m in range(4):
                        last = pe.transpose(PS[:, 6 + n % 2, m * P:(m + 1) * P], MN[:, n % 2, m * P:(m + 1) * P], ident[:])
                    last.then_inc(mod_turned, 1)

                for n in range(NPAN):
                    pe.wait_ge(panel_in[n % R], 16 * (n // R + 1))
                    if n >= 2:
                        pe.wait_ge(mod_out, n - 1)
                    for a in range(2):
                        for j in range(4):
                            last = pe.matmul(PS[32 * j:32 * j + 32, 4 + n % 2, :], CT[:, 2 * j + a, :], RING[:, n % R, 2 * j + a, :],
                                             start=(a == 0), stop=(a == 1))
                    last.then_inc(mod_done, 1)
                    if n:
                        turn(n - 1)
                turn(NPAN - 1)

            @block.vector
            def _(dve):
                for k in range(KT):
                    dve.wait_ge(x_turned, k + 1)
                    dve.tensor_copy(X[:, k, :], PS[:, k, 0:TOK]).then_inc(x_copied, 1)
                dve.wait_ge(ones_set, 2)
                dve.wait_ge(v_turned, 1)
                dve.tensor_copy(VT[:], PS[:, 0, 0:NV]).then_inc(v_copied, 1)
                dve.tensor_copy(ADAT[:], PS[:, 1, 0:NADA]).then_inc(v_copied, 1)
                dve.tensor_copy(CT[:, :, 0:NC_], PS[:, 2, 0:KT * NC_].rearrange("p (k c) -> p k c", c=NC_)).then_inc(v_copied, 1)
                dve.wait_ge(v_copied, 3)
                chain = Chain(dve, gs_chain)
                for n in range(NPAN):
                    dve.wait_ge(mod_turned, n + 1)
                    chain.link(dve.tensor_reduce(MS[:, n % 2], PS[:, 6 + n % 2, :].rearrange("p (m j c) -> p m c j", m=4, j=4)[:, :, 0:NC_, :],
                                                 AX.X, ALU.add))
                    dve.tensor_tensor(MOD[:, n // 12, 4 * (n % 12):4 * (n % 12) + 4, :], MS[:, n % 2],
                                      ADAT[:, 4 * n:4 * n + 4].unsqueeze(2).broadcast_to([P, 4, NC_]), ALU.add).then_inc(mod_set, 1)
                dve.wait_ge(mod_set, NPAN)
                for n in range(4):
                    l, w = n // 2, n % 2
                    chain.link(dve.tensor_scalar(GS[:, n], MOD[:, l, (3 * w + 1) * KT:(3 * w + 2) * KT, :], 1.0, None, ALU.add))
                    chain.link(dve.tensor_tensor(GS[:, n], GS[:, n],
                                                 VT[:, n * KT:(n + 1) * KT].unsqueeze(2).broadcast_to([P, KT, NC_]), ALU.mult))

    def norm_phase(which):
        SQ = sb(uniq("SQ"), [P, KT, TOK])
        RS = sb(uniq("RS"), [P, TOK])
        squared, summed, root_taken, rs_ready, chain_sem = (sem(uniq("squared")), sem(uniq("summed")), sem(uniq("root_taken")),
                                                            sem(uniq("rs_ready")), sem(uniq("norm_chain")))
        with nc.Block() as block:
            @block.scalar
            def _(act):
                for k in range(KT):
                    act.activation(SQ[:, k, :], X[:, k, :], ACT.Square).then_inc(squared, 1)
                act.wait_ge(rs_ready, 1)
                act.activation(RS[:], RS[:], ACT.Sqrt).then_inc(root_taken, 1)

            @block.tensor
            def _(pe):
                for k in range(KT):
                    pe.wait_ge(squared, k + 1)
                    last = pe.matmul(PS[:, 0, 0:TOK], ones[:], SQ[:, k, :], start=(k == 0), stop=(k == KT - 1))
                last.then_inc(summed, 1)

            @block.vector
            def _(dve):
                chain = Chain(dve, chain_sem)
                dve.wait_ge(summed, 1)
                dve.tensor_scalar(RS[:], PS[:, 0, 0:TOK], 1.0 / D, EPS, ALU.mult, ALU.add).then_inc(rs_ready, 1)
                dve.wait_ge(root_taken, 1)
                chain.link(dve.reciprocal(RS[:], RS[:]))
                chain.link(dve.tensor_tensor(H[:], X[:], RS[:].unsqueeze(1).broadcast_to([P, KT, TOK]), ALU.mult))
                if which == 4:
                    for k in range(KT):
                        chain.link(dve.tensor_scalar(H[:, k, :], H[:, k, :], VT[:, VOFF["final_g"] + k:VOFF["final_g"] + k + 1], None, ALU.mult))
                else:
                    l, w = which // 2, which % 2
                    shift = MOD[:, l, 3 * w * KT:(3 * w + 1) * KT, :]
                    for k in range(KT):
                        dve.tensor_scalar(H[:, k, 0:SEQ], H[:, k, 0:SEQ], GS[:, which, k, 0:1], shift[:, k, 0:1], ALU.mult, ALU.add)
                    hs = H[:, :, SEQ:].rearrange("p k (b t) -> p k b t", t=DT)
                    chain.link(dve.tensor_tensor(hs, hs, GS[:, which, :, 1:].unsqueeze(3).broadcast_to([P, KT, NB, DT]), ALU.mult))
                    chain.link(dve.tensor_tensor(hs, hs, shift[:, :, 1:].unsqueeze(3).broadcast_to([P, KT, NB, DT]), ALU.add))

    def project_phase(w, c0, cols, R, rhs, evac, split):
        RING = sb(uniq("w_ring"), [P, R, KT, 512])
        panel_in = [sem(uniq(f"panel_in{i}")) for i in range(R)]
        tile_done, out_v, out_s, chain_sem = sem(uniq("tile_done")), sem(uniq("out_v")), sem(uniq("out_s")), sem(uniq("out_chain"))
        panels = [(c, min(512, cols - c)) for c in range(0, cols, 512)]
        tiles = [(n, m, min(P, width - m)) for n, (c, width) in enumerate(panels) for m in range(0, width, P)]
        upto = [sum(1 for t in tiles if t[0] <= n) for n in range(len(panels))]
        B = 8
        with nc.Block() as block:
            @block.sync
            def _(sp):
                for n, (c, width) in enumerate(panels):
                    if n >= R:
                        sp.wait_ge(tile_done, upto[n - R])
                    sp.dma_start(RING[:, n % R, :, 0:width],
                                 w[:, c0 + c:c0 + c + width].rearrange("(k p) n -> p k n", p=P)).then_inc(panel_in[n % R], 16)

            @block.tensor
            def _(pe):
                for g, (n, m, width) in enumerate(tiles):
                    if m == 0:
                        pe.wait_ge(panel_in[n % R], 16 * (n // R + 1))
                    if g >= B:
                        if split and g % 2:
                            pe.wait_ge(out_s, (g - B) // 2 + 1)
                        else:
                            pe.wait_ge(out_v, (g - B) // 2 + 1 if split else g - B + 1)
                    for k in range(KT):
                        last = pe.matmul(PS[0:width, g % B, 0:TOK], RING[:, n % R, k, m:m + width], rhs[:, k, :],
                                         start=(k == 0), stop=(k == KT - 1))
                    last.then_inc(tile_done, 1)

            @block.vector
            def _(dve):
                chain = Chain(dve, chain_sem)
                for g, (n, m, width) in enumerate(tiles):
                    if not (split and g % 2):
                        if g and not split:
                            dve.wait_ge(out_v, g)
                        dve.wait_ge(tile_done, g + 1)
                        evac(dve, chain, g, PS[0:width, g % B, 0:TOK], width).then_inc(out_v, 1)

            @block.scalar
            def _(act):
                for g, (n, m, width) in enumerate(tiles):
                    if split and g % 2:
                        act.wait_ge(tile_done, g + 1)
                        evac(act, None, g, PS[0:width, g % B, 0:TOK], width).then_inc(out_s, 1)

    def copy_to(dst):
        def evac(eng, chain, g, psum, width):
            if chain is None:
                return eng.activation(dst[0:width, g, :], psum, ACT.Copy)
            return eng.tensor_copy(dst[0:width, g, :], psum)
        return evac

    def gated_residual(layer, which, tmp):
        gate = MOD[:, layer, (3 * which + 2) * KT:(3 * which + 3) * KT, :]

        def evac(dve, chain, g, psum, width):
            dve.scalar_tensor_tensor(X[:, g, 0:SEQ], psum[:, 0:SEQ], gate[:, g, 0:1], X[:, g, 0:SEQ], ALU.mult, ALU.add)
            chain.link(dve.tensor_tensor(tmp[:].rearrange("p (b t) -> p b t", t=DT),
                                         psum[:, SEQ:TOK].rearrange("p (b t) -> p b t", t=DT),
                                         gate[:, g, 1:].unsqueeze(2).broadcast_to([P, NB, DT]), ALU.mult))
            return dve.tensor_tensor(X[:, g, SEQ:TOK], X[:, g, SEQ:TOK], tmp[:], ALU.add)
        return evac

    def kv_rows_phase(QKV, NAT):
        R = 4
        turned, copied, stored = sem("kv_turned"), sem("kv_copied"), sem("kv_stored")
        units = [(t, j) for t in range(3) for j in range(4)]
        src = [4, 8, 16, 20]
        with nc.Block() as block:
            @block.tensor
            def _(pe):
                for u, (t, j) in enumerate(units):
                    n = P if t < 2 else NS
                    if u >= R:
                        pe.wait_ge(copied, u - R + 1)
                    for i in range(4):
                        last = pe.transpose(PS[0:n, u % R, i * P:(i + 1) * P], QKV[:, src[j] + i, t * P:t * P + n], ident[:])
                    last.then_inc(turned, 1)

            @block.vector
            def _(dve):
                for u, (t, j) in enumerate(units):
                    n = P if t < 2 else NS
                    dve.wait_ge(turned, u + 1)
                    dve.tensor_copy(NAT[0:n, t, j * 512:(j + 1) * 512], PS[0:n, u % R, :]).then_inc(copied, 1)

            @block.sync
            def _(sp):
                count = 0
                for m, mixer in enumerate(("win", "moba")):
                    for t in range(3):
                        n = P if t < 2 else NS
                        sp.wait_ge(copied, 4 * t + 2 * m + 2)
                        name = f"{mixer}_prompt" if t < 2 else f"{mixer}_sample"
                        rows = io[name].rearrange("b s a h e -> (b s) (a h e)")
                        rows = rows[t * P:(t + 1) * P, :] if t < 2 else rows
                        sp.dma_start(rows, NAT[0:n, t, m * 1024:(m + 1) * 1024]).then_inc(stored, 16)
                        count += 16
                sp.wait_ge(stored, count)

    def prompt_attention_phase(QKV, NAT):
        S = sb("pS", [P, 2, 384])
        PT = sb("pPT", [P, 2, 384])
        BIAS = sb("pBIAS", [P, 2, 384])
        negmax, denom, rden = sb("p_negmax", [P, 2, 2]), sb("p_denom", [P, 2, 2]), sb("p_rden", [P, 2, 2])
        bias_in, scored, maxed, exped, normed, turned, probs, mixed, stored, chain_sem = (
            sem(n) for n in ("p_bias_in", "p_scored", "p_maxed", "p_exped", "p_normed", "p_turned", "p_probs", "p_mixed",
                             "p_out", "p_chain"))
        heads = [(m, h) for m in range(2) for h in range(NH)]
        N = len(heads)
        parts = ((0, 0, P), (1, P, 2 * P))

        with nc.Block() as block:
            @block.sync
            def _(sp):
                sp.dma_start(BIAS[:], io["prompt_bias"]).then_inc(bias_in, 16)
                sp.wait_ge(bias_in, 16)

            @block.tensor
            def _(pe):
                for n in range(N + 2):
                    if n < N:
                        m, h = heads[n]
                        lo = 64 * (h % 2)
                        if n >= 2:
                            pe.wait_ge(maxed, n - 1)
                        for j, c, keys in parts:
                            last = pe.matmul(PS[:, n % 2, c:c + keys], QKV[lo:lo + 64, 12 * m + h // 2, j * P:(j + 1) * P],
                                             QKV[lo:lo + 64, 12 * m + 4 + h // 2, 0:keys], start=True, stop=True)
                        last.then_inc(scored, 1)
                    if 1 <= n <= N:
                        a = n - 1
                        pe.wait_ge(normed, a + 1)
                        if a >= 2:
                            pe.wait_ge(probs, a - 1)
                        for dst, src in ((0, 0), (P, P), (2 * P, 2 * P)):
                            last = pe.transpose(PS[:, 2 + a % 2, dst:dst + P], S[:, a % 2, src:src + P], ident[:])
                        last.then_inc(turned, 1)
                    if n >= 2:
                        a = n - 2
                        m, h = heads[a]
                        lo = 64 * (h % 2)
                        pe.wait_ge(probs, a + 1)
                        if a >= 2:
                            pe.wait_ge(stored, a - 1)
                        v = slice(m * 1024 + 512 + h * HD, m * 1024 + 512 + (h + 1) * HD)
                        out = PS[lo:lo + 64, 4 + a % 2, :]
                        pe.matmul(out[:, 0:P], NAT[:, 0, v], PT[:, a % 2, 0:P], start=True, stop=True)
                        pe.matmul(out[:, P:2 * P], NAT[:, 0, v], PT[:, a % 2, P:2 * P], start=True, stop=False)
                        pe.matmul(out[:, P:2 * P], NAT[:, 1, v], PT[:, a % 2, 2 * P:3 * P], start=False, stop=True).then_inc(mixed, 1)

            @block.vector
            def _(dve):
                chain = Chain(dve, chain_sem)
                dve.wait_ge(bias_in, 16)
                for n in range(N + 1):
                    if n < N:
                        if n >= 2:
                            dve.wait_ge(turned, n - 1)
                        dve.wait_ge(scored, n + 1)
                        s = n % 2
                        chain.link(dve.scalar_tensor_tensor(S[:, s, :], PS[:, s, 0:384], SCALE, BIAS[:, heads[n][0], :], ALU.mult, ALU.add))
                        dve.tensor_reduce(negmax[:, s, 0:1], S[:, s, 0:P], AX.X, ALU.max, negate=True)
                        dve.tensor_reduce(negmax[:, s, 1:2], S[:, s, P:384], AX.X, ALU.max, negate=True).then_inc(maxed, 1)
                    if n >= 1:
                        a = n - 1
                        s = a % 2
                        dve.wait_ge(exped, a + 1)
                        chain.link(dve.reciprocal(rden[:, s, :], denom[:, s, :]))
                        dve.tensor_scalar(S[:, s, 0:P], S[:, s, 0:P], rden[:, s, 0:1], None, ALU.mult)
                        dve.tensor_scalar(S[:, s, P:384], S[:, s, P:384], rden[:, s, 1:2], None, ALU.mult).then_inc(normed, 1)

            @block.scalar
            def _(act):
                for n in range(N + 2):
                    if n < N:
                        s = n % 2
                        act.wait_ge(maxed, n + 1)
                        if n >= 2:
                            act.wait_ge(normed, n - 1)
                        act.activation(S[:, s, 0:P], S[:, s, 0:P], ACT.Exp, bias=negmax[:, s, 0:1], accum_out=denom[:, s, 0:1])
                        act.activation(S[:, s, P:384], S[:, s, P:384], ACT.Exp, bias=negmax[:, s, 1:2],
                                       accum_out=denom[:, s, 1:2]).then_inc(exped, 1)
                    if 1 <= n <= N:
                        a = n - 1
                        act.wait_ge(turned, a + 1)
                        if a >= 2:
                            act.wait_ge(mixed, a - 1)
                        act.activation(PT[:, a % 2, :], PS[:, 2 + a % 2, 0:384], ACT.Copy).then_inc(probs, 1)
                    if n >= 2:
                        a = n - 2
                        m, h = heads[a]
                        lo = 64 * (h % 2)
                        act.wait_ge(mixed, a + 1)
                        act.activation(H[lo:lo + 64, 4 * m + h // 2, 0:SEQ], PS[lo:lo + 64, 4 + a % 2, 0:SEQ], ACT.Copy).then_inc(stored, 1)

    def sample_attention_phase(QS, NATS):
        KV = sb("KV", [P, SLOTS, 4, 512])
        KTT = sb("KTT", [P, 2, 2, 4, 512])
        NKEY = (NKA + NS, NKB + NS)
        SC = [sb("SCA", [P, NKEY[0]]), sb("SCB", [P, NKEY[1]])]
        NT = (TILES_A + 1, TILES_B + 1)
        PT = [sb("PTA", [P, NT[0], 2, 64]), sb("PTB", [P, NT[1], 2, 64])]
        QB = [sb("QBA", [P, 4, 2, 32]), sb("QBB", [P, 4, 2, 32])]
        OD = [sb("ODA", [P, 512]), sb("ODB", [P, 512])]
        WB = sb("WB", [P, NKA])
        NBIAS = sb("NBIAS", [P, 2, NB // 2, NS])
        HM = sb("HM", [P, 512])
        TSEL = sb("TSEL", [P, 2 * DT])
        TIE = sb("TIE", [P, 64])
        PTAB = sb("PTAB", [1, NPOOL], I32)
        G1, G2 = sb("G1", [P, 8, 8]), sb("G2", [P, 8, 8])
        bsum, rank = sb("bsum", [P, 8]), sb("rank", [P, 8])
        negmax, denom, rden = sb("s_negmax", [P, 2]), sb("s_denom", [P, 2]), sb("s_rden", [P, 2])

        consts_in, table_in, zeroed = sem("consts_in"), sem("table_in"), sem("zeroed")
        chunk_in = [[sem(f"{m}_chunk_in{i}") for i in range(SLOTS)] for m in ("A", "B", "B_odd")]
        v_used = sem("v_used")
        q_set = [sem("qA_set"), sem("qB_set")]
        k_turned, kt_s, kt_v = sem("k_turned"), sem("kt_s"), sem("kt_v")
        s_mm, s_out = sem("s_mm"), sem("s_out")
        maxed = [sem("A_maxed"), sem("B_maxed")]
        exped = [sem("A_exped"), sem("B_exped")]
        normed = [sem("A_normed"), sem("B_normed")]
        p_turned, p_out = sem("p_turned2"), sem("p_out2")
        od_done, o_turned, o_out = sem("od_done"), sem("o_turned"), sem("o_out")
        dve_chain = sem("s_dve_chain")
        waited = sem("pe_waited")

        far = io["cache_win_kv"][:, 0:FAR_TILES * 256].rearrange("b (i m r) a h e -> b a i m r (h e)", m=16, r=16)
        near = io["cache_win_kv"][:, FAR_TILES * 256:PAST].rearrange("b (i p) a h e -> b a i p (h e)", p=P)
        pool = io["cache_moba_kv"].rearrange("n p a h e -> n a p (h e)")
        sizes = (CHUNKS_A, CHUNKS_B)
        sizes2 = [[n for n in z for s in range(2)] for z in sizes]
        NPAIR = NB // 2
        LINKS = 9
        START, PER = len(sizes2[0]), 2 * (len(sizes2[0]) + len(sizes2[1]))
        assert PER == 4 * SLOTS
        IN = (64, 32, 32)
        FIRST_CHUNK = {("K", 1): 0, ("V", 0): 8, ("K", 0): 14, ("V", 1): 20}
        NKT, NBANK, NPT, NV_ = 2 * (TILES_A + TILES_B), 9, 8, 14
        KT0, S0 = (0, 2 * TILES_A), (0, 4)
        KBANK, PBANK, OBANK = (0, 1, 4), (5, 7), 6
        P0 = (0, 3)

        def ge(eng, semaphore, per, b, k):
            if isinstance(b, int):
                if per * b + k > 0:
                    eng.wait_ge(semaphore, per * b + k)
            else:
                eng.wait_ge(semaphore, b * per + k)

        def apart(pe):
            pe.sem_inc(waited, 1)

        with nc.Block() as block:
            def released(eng, b, c):
                if c < 0:
                    if isinstance(b, int) and b == 0:
                        if c >= -START:
                            eng.wait_ge(k_turned, sum(sizes2[0][0:START + c + 1]))
                        return
                    b, c = b - 1, c + PER
                elif isinstance(b, int) and b == NPAIR - 1 and c >= FIRST_CHUNK["K", 0]:
                    c += START
                for (kv, mixer), first in FIRST_CHUNK.items():
                    j = c - first
                    if 0 <= j < len(sizes2[mixer]):
                        if kv == "V":
                            ge(eng, v_used, NV_, b, len(sizes2[0]) * mixer + j + 1)
                        else:
                            ge(eng, k_turned, NKT, b, (NKT, KT0[1])[mixer] + sum(sizes2[mixer][0:j + 1]))

            def load_body(eng, load, b, last):
                for kv, mixer in ((0, 1), (1, 0), (0, 0), (1, 1)):
                    ahead = (kv, mixer) == (0, 0)
                    if last and ahead:
                        continue
                    c0 = FIRST_CHUNK["KV"[kv], mixer] - (START if last and kv == 1 and mixer == 1 else 0)
                    for j in range(len(sizes2[mixer])):
                        n = START + c0 + j
                        load(kv, mixer, (b + 1 if ahead else b) * 2 + j % 2, j // 2, n % SLOTS,
                             lambda b=b, c=c0 + j - SLOTS: released(eng, b, c))

            def load_bodies(eng, load):
                load_body(eng, load, 0, False)
                with eng.Fori(1, NPAIR - 1) as b:
                    load_body(eng, load, b, False)
                load_body(eng, load, NPAIR - 1, True)

            def load_pages(eng, kv, b, chunk, slot, when_free, odd):
                tiles = range(odd, CHUNKS_B[chunk], 2)
                pages = [eng.value_load(PTAB[0:1, bass.ds(b * NPAGE + 4 * chunk + x, 1)], min_val=0, max_val=NPOOL - 1) for x in tiles]
                when_free()
                for x, page in zip(tiles, pages):
                    eng.dma_start(KV[:, slot, x, :], pool[bass.ds(page, 1), kv].rearrange("o p n -> (o p) n")).then_inc(chunk_in[1 + odd][slot], 16)

            @block.gpsimd
            def _(gp):
                def load(kv, mixer, b, chunk, slot, when_free):
                    if mixer == 1:
                        load_pages(gp, kv, b, chunk, slot, when_free, 1)

                gp.wait_ge(table_in, 16)
                load_bodies(gp, load)

            @block.sync
            def _(sp):
                def load(kv, mixer, b, chunk, slot, when_free):
                    if mixer == 1:
                        load_pages(sp, kv, b, chunk, slot, when_free, 0)
                        return
                    first, n = 4 * chunk, CHUNKS_A[chunk]
                    when_free()
                    parts = 4 // n
                    for t in range(first, first + n):
                        for q in range(parts):
                            rows = P // parts
                            if t < FAR_TILES:
                                src = far[bass.ds(b, 1), kv, t, :, 0:8].rearrange("o m r n -> (o m) r n")
                            else:
                                src = near[bass.ds(b, 1), kv, t - FAR_TILES, q * rows:(q + 1) * rows].rearrange("o p n -> (o p) n")
                            sp.dma_start(KV[q * rows:(q + 1) * rows, slot, t - first, :], src).then_inc(chunk_in[0][slot], 16)

                sp.dma_start(PTAB[0:1, 0:NB * NPAGE], io["page_table"].rearrange("b n -> (b n)").rearrange("(o n) -> o n", o=1)).then_inc(table_in, 16)
                for j in range(START):
                    load(0, 0, j % 2, j // 2, j, lambda: None)
                for dst, name in ((WB, "win_bias"), (NBIAS, "new_bias"), (HM, "head_mask"), (TSEL, "token_select"), (TIE, "tie")):
                    sp.dma_start(dst[:], io[name]).then_inc(consts_in, 16)
                sp.wait_ge(table_in, 16)
                load_bodies(sp, load)

            @block.tensor
            def _(pe):
                def slot_of(kv, m, b, chunk, s, last):
                    j = 2 * chunk + s
                    if b is None:
                        pe.wait_ge(chunk_in[0][j], IN[0])
                        return j
                    n = START + FIRST_CHUNK[kv, m] + j - (START if last and (kv, m) == ("V", 1) else 0)

                    def count(end, last):
                        mixers = [1] * len(sizes2[1]) + [0] * len(sizes2[0]) * (1 if last else 2) + [1] * len(sizes2[1])
                        return sum(mixers[i] == m and (START + i - n) % SLOTS == 0 for i in range(end))

                    start = int(m == 0 and n % SLOTS < START)
                    for q in range(m, 2 * m + 1):
                        ge(pe, chunk_in[q][n % SLOTS], IN[q] * count(PER, False), b, IN[q] * (start + count(n - START + 1, last)))
                    return n % SLOTS

                def keys(m, b, body, last, between):
                    ge(pe, q_set[m], 1, b, 1)

                    def scores(q, rhs, width):
                        ge(pe, s_out, NBANK, b, S0[m] + max(q - 1, 0))
                        for s in range(2):
                            for i in range(4):
                                mm = pe.matmul(PS[32 * i:32 * i + 32, 2 + q % 2, 0:width], QB[m][:, i, s, :], rhs(s)[:, i, 0:width],
                                               start=(s == 0), stop=(s == 1))
                        mm.then_inc(s_mm, 1)

                    def chunk_scores(c):
                        done = sum(sizes[m][0:c + 1])
                        ge(pe, kt_s, NKT // 2, b, KT0[m] // 2 + done)
                        ge(pe, kt_v, NKT // 2, b, KT0[m] // 2 + done)
                        scores(c + 1, lambda s: KTT[:, c % 2, s], sizes[m][c] * P)

                    t = 0
                    for chunk, n in enumerate(sizes[m]):
                        for s in range(2):
                            slot = slot_of("K", m, body, chunk, s, last)
                            for x in range(n):
                                if t >= 3:
                                    ge(pe, (kt_s, kt_v)[(t - 3) % 2], NKT // 2, b, KT0[m] // 2 + (t - 3) // 2 + 1)
                                for i in range(4):
                                    tr = pe.transpose(PS[:, KBANK[t % 3], i * P:(i + 1) * P], KV[:, slot, x, i * P:(i + 1) * P], ident[:])
                                tr.then_inc(k_turned, 1)
                                t += 1
                        if chunk == 0:
                            scores(0, lambda s: QS[:, 12 * m + 4:12 * m + 8, :], NS)
                        else:
                            chunk_scores(chunk - 1)
                    between()
                    chunk_scores(len(sizes[m]) - 1)

                def probabilities(m, b):
                    ge(pe, normed[m], 1, b, 1)
                    for j in range(-(-NT[m] // 4)):
                        ge(pe, p_out, NPT, b, P0[m] + max(j - 1, 0))
                        apart(pe)
                        for t in range(4 * j, min(4 * j + 4, NT[m])):
                            n = P if t < NT[m] - 1 else NS
                            tr = pe.transpose(PS[0:n, PBANK[j % 2], (t % 4) * P:(t % 4 + 1) * P], SC[m][:, t * P:t * P + n], ident[:])
                        tr.then_inc(p_turned, 1)

                def values(m, b, last):
                    ge(pe, o_out, 2, b, m)
                    ge(pe, p_out, NPT, b, (P0[1], NPT)[m])
                    apart(pe)

                    def product(rows, t, s, v, start, stop):
                        return pe.matmul(PS[64 * s:64 * s + 64, OBANK, :], PT[m][0:rows, t, s, :], v, start=start, stop=stop)

                    for s in range(2):
                        product(64, NT[m] - 1, s, NATS[:, m * 1024 + 512:(m + 1) * 1024], True, False)
                    for chunk, n in enumerate(sizes[m]):
                        slots = [slot_of("V", m, b, chunk, s, last) for s in range(2)]
                        end = chunk == len(sizes[m]) - 1
                        for x in range(n):
                            for s in range(2):
                                mm = product(P, 4 * chunk + x, s, KV[:, slots[s], x, :], False, end and x == n - 1)
                                if x == n - 1:
                                    mm.then_inc(v_used, 1)

                def outputs(m, b, back=0):
                    ge(pe, od_done, 2, b, m + 1 - 2 * back)
                    apart(pe)
                    for i in range(4):
                        mm = pe.matmul(PS[:, OBANK, i * 2 * DT:(i + 1) * 2 * DT], OD[m][:, i * P:(i + 1) * P], TSEL[:], start=True, stop=True)
                    mm.then_inc(o_turned, 1)

                def body(b, last):
                    if isinstance(b, int) and b == 0:
                        pe.wait_ge(consts_in, 80)

                    def before_a():
                        probabilities(0, b)
                        if not (isinstance(b, int) and b == 0):
                            outputs(1, b, 1)

                    def before_b():
                        probabilities(1, b)
                        outputs(0, b)

                    keys(1, b, b, last, before_a)
                    values(0, b, last)
                    if last:
                        before_b()
                    else:
                        keys(0, b + 1, b, last, before_b)
                    values(1, b, last)
                    if last:
                        outputs(1, b)

                keys(0, 0, None, False, lambda: None)
                body(0, False)
                with pe.Fori(1, NPAIR - 1) as b:
                    body(b, False)
                body(NPAIR - 1, True)

            def copy_keys(eng, copy, parity, done, m, b, chunk):
                ge(eng, s_mm, NBANK, b, S0[m] + (chunk if chunk >= 2 else 0))
                for s, x in [(s, x) for s in range(2) for x in range(parity, sizes[m][chunk], 2)]:
                    t = 8 * chunk + s * sizes[m][chunk] + x
                    ge(eng, k_turned, NKT, b, KT0[m] + t + 1)
                    copy(KTT[:, chunk % 2, s, :, x * P:(x + 1) * P], PS[:, KBANK[t % 3], :].rearrange("p (i n) -> p i n", n=P)).then_inc(done, 1)

            @block.scalar
            def _(act):
                def copy(out, in_):
                    return act.activation(out, in_, ACT.Copy)

                def keys(m, b):
                    for chunk in range(len(sizes[m])):
                        copy_keys(act, copy, 0, kt_s, m, b, chunk)

                def exp(m, b):
                    ge(act, maxed[m], 1, b, 1)
                    act.activation(SC[m][:], SC[m][:], ACT.Exp, bias=negmax[:, m:m + 1], accum_out=denom[:, m:m + 1]).then_inc(exped[m], 1)

                def probabilities(m, b):
                    for j in range(-(-NT[m] // 4)):
                        ge(act, p_turned, NPT, b, P0[m] + j + 1)
                        t0, t1 = 4 * j, min(4 * j + 4, NT[m] - 1)
                        bank = PS[:, PBANK[j % 2], :].rearrange("k (t i s x) -> k t s i x", t=4, i=4, s=2)
                        for s in range(2):
                            if t1 > t0:
                                last = copy(PT[m][:, t0:t1, s, :].rearrange("k t (i x) -> k t i x", i=4), bank[:, 0:t1 - t0, s])
                            if j == -(-NT[m] // 4) - 1:
                                last = copy(PT[m][0:64, NT[m] - 1, s, :].rearrange("k (i x) -> k i x", i=4), bank[0:64, (NT[m] - 1) % 4, s])
                        last.then_inc(p_out, 1)

                def outputs(m, b, back=0):
                    ge(act, o_turned, 2, b, m + 1 - 2 * back)
                    n = 2 * DT
                    where = bass.ds(b * n + (SEQ - n * back), n)
                    copy(H[:, 4 * m:4 * m + 4, where], PS[:, OBANK, 0:4 * n].rearrange("p (i t) -> p i t", t=n)).then_inc(o_out, 1)

                def body(b, last):
                    keys(1, b)
                    probabilities(0, b)
                    if not (isinstance(b, int) and b == 0):
                        outputs(1, b, 1)
                    exp(1, b)
                    if not last:
                        keys(0, b + 1)
                    probabilities(1, b)
                    outputs(0, b)
                    if not last:
                        exp(0, b + 1)
                    else:
                        outputs(1, b)

                keys(0, 0)
                exp(0, 0)
                body(0, False)
                with act.Fori(1, NPAIR - 1) as b:
                    body(b, False)
                body(NPAIR - 1, True)

            @block.vector
            def _(dve):
                chain = Chain(dve, dve_chain)

                def queries(m, b):
                    ge(dve, s_mm, NBANK, b, S0[m] - NBANK + (4, 5)[m])
                    for half, s in ((0, 0), (0, 1), (1, 0), (1, 1)):
                        rows, first = slice(64 * half, 64 * half + 64), 16 * s + DT * half
                        where = bass.ds(b * (2 * DT) + s * DT, DT)
                        last = dve.tensor_copy(QB[m][rows, :, s, first:first + DT], QS[rows, 12 * m:12 * m + 4, where])
                    last.then_inc(q_set[m], 1)

                def keys(m, b):
                    ge(dve, p_turned, NPT, b, (P0[1], NPT)[m] - NPT)
                    nk = (NKA, NKB)[m]

                    def scores(q):
                        ge(dve, s_mm, NBANK, b, S0[m] + q + 1)
                        if q == 0:
                            bias = NBIAS[:, m, b, :] if isinstance(b, int) else NBIAS[:, m, bass.ds(b, 1), :].rearrange("p o n -> p (o n)")
                            dst, src = SC[m][:, nk:nk + NS], PS[:, 2, 0:NS]
                        else:
                            c0, width = 512 * (q - 1), sizes[m][q - 1] * P
                            dst, src = SC[m][:, c0:c0 + width], PS[:, 2 + q % 2, 0:width]
                            bias = WB[:, c0:c0 + width] if m == 0 else None
                        if q == 0 or m == 0:
                            last = dve.scalar_tensor_tensor(dst, src, SCALE, bias, ALU.mult, ALU.add)
                        else:
                            last = dve.tensor_scalar(dst, src, SCALE, None, ALU.mult)
                        last.then_inc(s_out, 1)

                    for chunk in range(len(sizes[m])):
                        copy_keys(dve, dve.tensor_copy, 1, kt_v, m, b, chunk)
                        scores(chunk)
                    scores(len(sizes[m]))
                    ge(dve, s_out, NBANK, b, S0[m] + len(sizes[m]) + 1)
                    if m == 1:
                        blocks = SC[1][:, 0:NKB].rearrange("p (n k) -> p n k", k=256)
                        chain.link(dve.tensor_reduce(bsum[:], blocks, AX.X, ALU.add))
                        theirs, own = bsum[:].unsqueeze(1).broadcast_to([P, 8, 8]), bsum[:].unsqueeze(2).broadcast_to([P, 8, 8])
                        dve.tensor_tensor(G1[:], theirs, own, ALU.is_gt)
                        chain.link(dve.tensor_tensor(G2[:], theirs, own, ALU.is_equal))
                        chain.link(dve.tensor_tensor(G2[:], G2[:], TIE[:].rearrange("p (i j) -> p i j", j=8), ALU.mult))
                        chain.link(dve.tensor_tensor(G1[:], G1[:], G2[:], ALU.add))
                        chain.link(dve.tensor_reduce(rank[:], G1[:], AX.X, ALU.add))
                        chain.link(dve.tensor_scalar(rank[:], rank[:], 2.5, NEG, ALU.is_gt, ALU.mult))
                        chain.link(dve.tensor_tensor(blocks, blocks, rank[:].unsqueeze(2).broadcast_to([P, 8, 256]), ALU.add))
                    dve.tensor_reduce(negmax[:, m:m + 1], SC[m][:], AX.X, ALU.max, negate=True).then_inc(maxed[m], 1)

                def normalise(m, b):
                    ge(dve, exped[m], 1, b, 1)
                    chain.link(dve.reciprocal(rden[:, m:m + 1], denom[:, m:m + 1]))
                    dve.tensor_scalar(SC[m][:], SC[m][:], rden[:, m:m + 1], None, ALU.mult).then_inc(normed[m], 1)

                def own_head(m, b):
                    ge(dve, v_used, NV_, b, (len(sizes2[0]), NV_)[m])
                    ge(dve, o_turned, 2, b, m - 1)
                    dve.tensor_tensor(OD[m][:], PS[:, OBANK, :], HM[:], ALU.mult).then_inc(od_done, 1)

                def body(b, last):
                    normalise(0, b)
                    queries(1, b)
                    keys(1, b)
                    normalise(1, b)
                    own_head(0, b)
                    if not last:
                        queries(0, b + 1)
                        keys(0, b + 1)
                    own_head(1, b)

                dve.memset(QB[0][:], 0.0).then_inc(zeroed, 1)
                dve.memset(QB[1][:], 0.0).then_inc(zeroed, 1)
                dve.wait_ge(zeroed, 2)
                queries(0, 0)
                dve.wait_ge(consts_in, 80)
                keys(0, 0)
                body(0, False)
                with dve.Fori(1, NPAIR - 1) as b:
                    chain.enter(b - 1, LINKS)
                    body(b, False)
                    chain.leave(NPAIR - 2)
                body(NPAIR - 1, True)

    def keep_samples_phase(QKV, NAT, QS, NATS):
        kept = sem("kept")
        with nc.Block() as block:
            @block.vector
            def _(dve):
                dve.tensor_copy(QS[:], QKV[:, :, SEQ:TOK]).then_inc(kept, 1)

            @block.scalar
            def _(act):
                act.activation(NATS[:], NAT[0:NS, 2, :], ACT.Copy).then_inc(kept, 1)

    def residual_phase(w, rhs, layer):
        tmp = sb(uniq("residual_tmp"), [P, NS])
        project_phase(w, 0, D, 3, rhs, gated_residual(layer, 0, tmp), False)

    def clear_phase(where):
        cleared = sem(uniq("cleared"))
        with nc.Block() as block:
            @block.vector
            def _(dve):
                dve.memset(where, 0.0).then_inc(cleared, 1)

    def swiglu_engines(R, RING, HT, T1, T2, panel_in, up_done, down_done, silu_done, hid_done, hid_banks, acc_done):
        UPC = [(c, min(512, DFF - c)) for c in range(0, DFF, 512)]
        NUP = 2 * len(UPC)
        DOWN = [(half, k, min(8, FT - k)) for half in range(2) for k in range(0, FT, 8)]
        NPAN = NUP + len(DOWN)
        assert NPAN % R == 0

        def ge(eng, semaphore, per, e, k):
            if isinstance(e, int):
                if per * e + k > 0:
                    eng.wait_ge(semaphore, per * e + k)
            elif isinstance(e, tuple):
                eng.wait_ge(semaphore, e[0] * per + (per + k))
            else:
                eng.wait_ge(semaphore, e * per + k)

        def loads(sp, e, w1, w3, w2):
            for n in range(NPAN):
                s = n % R
                back = n - R
                if back < 0:
                    ge(sp, down_done, len(DOWN), e, back + R - len(DOWN) + 1)
                elif back < NUP:
                    ge(sp, up_done, FT, e, min(4 * (back // 2 + 1), FT))
                else:
                    ge(sp, down_done, len(DOWN), e, back - NUP + 1)
                if n < NUP:
                    c, width = UPC[n // 2]
                    src = (w1, w3)[n % 2][:, c:c + width].rearrange("(k p) n -> p k n", p=P)
                    sp.dma_start(RING[:, s, :, 0:width], src).then_inc(panel_in[s], 16)
                else:
                    half, k, nk = DOWN[n - NUP]
                    src = w2[k * P:(k + nk) * P, half * 512:(half + 1) * 512].rearrange("(k p) n -> p k n", p=P)
                    sp.dma_start(RING[:, s, 0:nk, :], src).then_inc(panel_in[s], 16)

        def arrived(pe, e, n):
            ge(pe, panel_in[n % R], 16 * (NPAN // R), e, 16 * (n // R + 1))

        def products(pe, e, rhs):
            for f in range(FT):
                n, m = 2 * (f // 4), f % 4
                if m == 0:
                    arrived(pe, e, n)
                    arrived(pe, e, n + 1)
                ge(pe, hid_banks, FT, e, f - 1)
                for w in range(2):
                    for k in range(KT):
                        mm = pe.matmul(PS[:, 2 * (f % 2) + w, 0:TOK], RING[:, (n + w) % R, k, m * P:(m + 1) * P], rhs[:, k, :],
                                       start=(k == 0), stop=(k == KT - 1))
                mm.then_inc(up_done, 1)
            for d, (half, k0, nk) in enumerate(DOWN):
                n = NUP + d
                arrived(pe, e, n)
                if k0 == 0:
                    ge(pe, acc_done, KT, e, 4 * half)
                ge(pe, hid_done, FT, e, k0 + nk)
                for o in range(4):
                    for k in range(nk):
                        mm = pe.matmul(PS[:, 4 + o, 0:TOK], RING[:, n % R, k, o * P:(o + 1) * P], HT[:, k0 + k, :],
                                       start=(k0 + k == 0), stop=(k0 + k == FT - 1))
                mm.then_inc(down_done, 1)

        def silus(act, e):
            for f in range(FT):
                ge(act, up_done, FT, e, f + 1)
                ge(act, hid_done, FT, e, f - 1)
                act.activation(T1[:, f % 2, :], PS[:, 2 * (f % 2), 0:TOK], ACT.Silu).then_inc(silu_done, 1)

        def hidden(dve, e, gate):
            for f in range(FT):
                if f == 0:
                    ge(dve, down_done, len(DOWN), e, 0)
                ge(dve, silu_done, FT, e, f + 1)
                if gate is None:
                    dve.tensor_tensor(HT[:, f, :], T1[:, f % 2, :], PS[:, 2 * (f % 2) + 1, 0:TOK], ALU.mult).then_inc(hid_done, 1)
                else:
                    dve.tensor_tensor(T2[:, f % 2, :], gate, PS[:, 2 * (f % 2) + 1, 0:TOK], ALU.mult).then_inc(hid_banks, 1)
                    ge(dve, hid_banks, FT, e, f + 1)
                    dve.tensor_tensor(HT[:, f, :], T1[:, f % 2, :], T2[:, f % 2, :], ALU.mult).then_inc(hid_done, 1)

        return loads, products, silus, hidden, ge

    def dense_phase():
        R = 6
        RING = sb("ffn_ring", [P, R, KT, 512])
        HT = sb("ffn_hidden", [P, FT, TOK])
        T1, tmp = sb("ffn_silu", [P, 2, TOK]), sb("ffn_tmp", [P, NS])
        panel_in = [sem(f"ffn_in{i}") for i in range(R)]
        up_done, down_done, silu_done, hid_done, acc_done = (sem("ffn_" + n) for n in ("up_done", "down_done", "silu_done", "hid_done", "acc_done"))
        loads, products, silus, hidden, ge = swiglu_engines(R, RING, HT, T1, None, panel_in, up_done, down_done, silu_done,
                                                            hid_done, hid_done, acc_done)
        chain_sem = sem("ffn_chain")
        evac = gated_residual(0, 1, tmp)
        with nc.Block() as block:
            @block.sync
            def _(sp):
                loads(sp, 0, io["ffn_w1"], io["ffn_w3"], io["ffn_w2"])

            @block.tensor
            def _(pe):
                products(pe, 0, H)

            @block.scalar
            def _(act):
                silus(act, 0)

            @block.vector
            def _(dve):
                chain = Chain(dve, chain_sem)
                hidden(dve, 0, None)
                for half in range(2):
                    dve.wait_ge(down_done, 3 * (half + 1))
                    for o in range(4):
                        g = 4 * half + o
                        if g:
                            dve.wait_ge(acc_done, g)
                        evac(dve, chain, g, PS[:, 4 + o, 0:TOK], P).then_inc(acc_done, 1)

    def retention_phase(DD, Y):
        COS, SIN, ROT = sb("COS", [P, TOK]), sb("SIN", [P, TOK]), sb("ROT", [P, P])
        QDEC, KDEC = sb("QDEC", [P, NHD, TOK]), sb("KDEC", [P, 3, NHD])
        DMASK, DMASKS = sb("DMASK", [P, NHD, P]), sb("DMASKS", [NS, NHD, NS])
        BMASK, CDEC = sb("BMASK", [NS, NB]), sb("CDEC", [P, 2, NHD])
        RS, RN = sb("RS_old", [P, NB, NHD, P]), sb("RS_new", [P, NB, NHD, P])
        TMP, QD = sb("d_tmp", [P, 8, TOK]), sb("QD", [P, NHD, TOK])
        KN, VN, KM = sb("d_KN", [P, 3, NHD, P]), sb("d_VN", [P, 3, NHD * P]), sb("d_KM", [NS, NB, NHD * P])
        ST, STS = sb("ST_d", [P, NHD, 2, P]), sb("STS_d", [NS, NHD, NS])
        R1, R2 = sb("R1", [P, NHD, P]), sb("R2", [P, NHD, P])
        names_ = ("d_tables", "d_states", "d_rot", "d_rotated", "d_turned", "d_rows", "d_km", "d_scored", "d_masked", "d_r1", "d_r1out",
                  "d_r2", "d_new", "d_newout", "d_o", "d_sq", "d_sum", "d_rs", "d_root", "d_gate", "d_stored", "d_chain", "d_r2out")
        (tables, states, rot, rotated, turned, rows, km, scored, masked, r1, r1out, r2, new, newout, o_done, sq, summed, rs,
         rooted, gated, stored, chain_sem, r2out) = (sem(n) for n in names_)
        with nc.Block() as block:
            @block.sync
            def _(sp):
                for dst, name in ((COS, "cos"), (SIN, "sin"), (ROT, "rotate"), (QDEC, "q_dec"), (KDEC, "k_dec"), (DMASK, "d_mask"),
                                  (DMASKS, "d_mask_sample"), (BMASK, "sample_mask"), (CDEC, "chunk_dec")):
                    sp.dma_start(dst[:], io[name]).then_inc(tables, 16)
                for b in range(NB):
                    sp.dma_start(RS[:, b], io["state_ret"][b].rearrange("h e f -> e h f")).then_inc(states, 16)
                sp.wait_ge(r2out, NHD)
                sp.dma_start(io["ret_prompt"].rearrange("o h e f -> e (o h) f"), R2[:]).then_inc(stored, 16)
                sp.wait_ge(newout, NB)
                sp.dma_start(io["ret_sample"].rearrange("b h e f -> e b h f"), RN[:]).then_inc(stored, 16)
                sp.wait_ge(stored, 32)

            @block.tensor
            def _(pe):
                pe.wait_ge(tables, 144)
                for i in range(8):
                    mm = pe.matmul(PS[:, i, 0:TOK], ROT[:], DD[:, i, :], start=True, stop=True)
                mm.then_inc(rot, 1)
                pe.wait_ge(rotated, 1)
                for t in range(3):
                    n = P if t < 2 else NS
                    for kv in range(2):
                        for h in range(NHD):
                            mm = pe.transpose(PS[0:n, 3 * kv + t, h * P:(h + 1) * P], DD[:, 4 + 4 * kv + h, t * P:t * P + n], ident[:])
                mm.then_inc(turned, 1)
                pe.wait_ge(rows, 6)
                for h in range(NHD):
                    for c in range(2):
                        pe.matmul(PS[:, h, c * P:(c + 1) * P], DD[:, 4 + h, c * P:(c + 1) * P], DD[:, h, c * P:(c + 1) * P], start=True, stop=True)
                    mm = pe.matmul(PS[0:NS, h, SEQ:TOK], DD[:, 4 + h, SEQ:TOK], DD[:, h, SEQ:TOK], start=True, stop=True)
                mm.then_inc(scored, 1)
                for c in range(2):
                    for h in range(NHD):
                        mm = pe.matmul(PS[:, 4 + c, h * P:(h + 1) * P], KN[:, c, h, :], VN[:, c, h * P:(h + 1) * P], start=True, stop=True)
                mm.then_inc(r1, 1)
                pe.wait_ge(km, 8)
                for b in range(NB):
                    if b >= 2:
                        pe.wait_ge(newout, b - 1)
                    for h in range(NHD):
                        mm = pe.matmul(PS[:, 6 + b % 2, h * P:(h + 1) * P], KM[:, b, h * P:(h + 1) * P], VN[0:NS, 2, h * P:(h + 1) * P], start=True, stop=True)
                    mm.then_inc(new, 1)
                pe.wait_ge(masked, 2)
                pe.wait_ge(r1out, 1)
                pe.wait_ge(states, 16 * NB)
                for h in range(NHD):
                    out = PS[:, h, :]
                    pe.matmul(out[:, 0:P], VN[:, 0, h * P:(h + 1) * P], ST[:, h, 0, :], start=True, stop=True)
                    pe.matmul(out[:, P:2 * P], VN[:, 1, h * P:(h + 1) * P], ST[:, h, 1, :], start=True, stop=False)
                    pe.matmul(out[:, P:2 * P], R1[:, h, :], QD[:, h, P:2 * P], start=False, stop=True)
                    pe.matmul(out[:, SEQ:TOK], VN[0:NS, 2, h * P:(h + 1) * P], STS[:, h, :], start=True, stop=False)
                    for b in range(NB):
                        mm = pe.matmul(out[:, SEQ + DT * b:SEQ + DT * (b + 1)], RS[:, b, h, :], QD[:, h, SEQ + DT * b:SEQ + DT * (b + 1)],
                                       start=False, stop=(b == NB - 1))
                mm.then_inc(o_done, 1)
                pe.wait_ge(r2out, NHD)
                pe.wait_ge(newout, NB)
                for h in range(NHD):
                    pe.wait_ge(sq, h + 1)
                    mm = pe.matmul(PS[:, 4 + h, 0:TOK], ones[:], TMP[:, h, :], start=True, stop=True)
                mm.then_inc(summed, 1)

            @block.scalar
            def _(act):
                act.activation(DD[:, 12:16, :], DD[:, 12:16, :], ACT.Silu).then_inc(gated, 1)
                act.wait_ge(o_done, 1)
                for h in range(NHD):
                    act.activation(TMP[:, h, :], PS[:, h, 0:TOK], ACT.Square).then_inc(sq, 1)
                act.wait_ge(rs, 1)
                act.activation(TMP[:, 4:8, :], TMP[:, 4:8, :], ACT.Sqrt).then_inc(rooted, 1)

            @block.vector
            def _(dve):
                chain = Chain(dve, chain_sem)
                dve.wait_ge(tables, 144)
                dve.wait_ge(rot, 1)
                wide = [P, 8, TOK]
                dve.tensor_tensor(TMP[:], PS[:, :, 0:TOK], SIN[:].unsqueeze(1).broadcast_to(wide), ALU.mult)
                chain.link(dve.tensor_tensor(DD[:, 0:8, :], DD[:, 0:8, :], COS[:].unsqueeze(1).broadcast_to(wide), ALU.mult))
                dve.tensor_tensor(DD[:, 0:8, :], DD[:, 0:8, :], TMP[:], ALU.add).then_inc(rotated, 1)
                dve.wait_ge(rotated, 1)
                chain.link(dve.tensor_tensor(QD[:], DD[:, 0:4, :], QDEC[:], ALU.mult))
                dve.wait_ge(turned, 1)
                for t in range(3):
                    n = P if t < 2 else NS
                    dve.tensor_tensor(KN[0:n, t], PS[0:n, t, :].rearrange("p (h e) -> p h e", e=P),
                                      KDEC[0:n, t, :].unsqueeze(2).broadcast_to([n, NHD, P]), ALU.mult).then_inc(rows, 1)
                    dve.tensor_copy(VN[0:n, t, :], PS[0:n, 3 + t, :]).then_inc(rows, 1)
                dve.wait_ge(rows, 6)
                for b in range(NB):
                    dve.tensor_scalar(KM[:, b, :], KN[0:NS, 2].rearrange("p h e -> p (h e)"), BMASK[:, b:b + 1], None, ALU.mult).then_inc(km, 1)
                dve.wait_ge(scored, 1)
                dve.tensor_tensor(ST[:], PS[:, 0:4, 0:SEQ].rearrange("p h (c q) -> p h c q", q=P),
                                  DMASK[:].unsqueeze(2).broadcast_to([P, NHD, 2, P]), ALU.mult).then_inc(masked, 1)
                dve.tensor_tensor(STS[:], PS[0:NS, 0:4, SEQ:TOK], DMASKS[:], ALU.mult).then_inc(masked, 1)
                dve.wait_ge(r1, 1)
                dve.tensor_copy(R1[:], PS[:, 4, :].rearrange("p (h e) -> p h e", e=P)).then_inc(r1out, 1)
                dve.wait_ge(r1out, 1)
                for h in range(NHD):
                    dve.scalar_tensor_tensor(R2[:, h, :], R1[:, h, :], CDEC[:, 0, h:h + 1], PS[:, 5, h * P:(h + 1) * P], ALU.mult, ALU.add).then_inc(r2out, 1)
                dve.wait_ge(states, 16 * NB)
                for h in range(NHD):
                    last = dve.tensor_scalar(RN[:, :, h, :], RS[:, :, h, :], CDEC[:, 1, h:h + 1], None, ALU.mult)
                chain.link(last)
                for b in range(NB):
                    dve.wait_ge(new, b + 1)
                    dve.tensor_tensor(RN[:, b], RN[:, b], PS[:, 6 + b % 2, :].rearrange("p (h e) -> p h e", e=P), ALU.add).then_inc(newout, 1)
                dve.wait_ge(summed, 1)
                dve.tensor_scalar(TMP[:, 4:8, :], PS[:, 4:8, 0:TOK], 1.0 / HDD, EPS, ALU.mult, ALU.add).then_inc(rs, 1)
                dve.wait_ge(rooted, 1)
                chain.link(dve.reciprocal(TMP[:, 4:8, :], TMP[:, 4:8, :]))
                chain.link(dve.tensor_tensor(Y[:, 4:8, :], PS[:, 0:4, 0:TOK], TMP[:, 4:8, :], ALU.mult))
                dve.wait_ge(gated, 1)
                chain.link(dve.tensor_tensor(Y[:, 4:8, :], Y[:, 4:8, :], DD[:, 12:16, :], ALU.mult))

    def rwkv_prepare_phase(PC, AR, BK, VS, G, BON, PEND):
        PREV = sb("PREV", [P, 15, TOK])
        SSN, SST = sb("SSN", [NB, C_COLS]), sb("SST", [P, 15, NB])
        LAST, LASTN = sb("LAST", [P, 15, NC_]), sb("LASTN", [NC_, C_COLS])
        WUP, GUP = sb("WUP", [P, W_MIX]), sb("GUP", [P, 2, W_MIX])
        BO, RESET = sb("BO", [P, P]), sb("RESET", [P, TOK])
        LD, AA, KK, T4, T5 = (sb(n, [P, 4, TOK]) for n in ("LD", "AA", "KK", "T4", "T5"))
        SG = sb("SG", [P, 3, TOK])
        (loaded, turned_in, sst_out, last_set, turned_out, lastn_out, stored, mixed, loras_in, lora, lora2, lora_out, lora_free, norms_in,
         norm_mm, norm_rooted, norm_rd, rk_in, rk_mm, cums, exps, cdiff, used, chain_sem, act_chain, zeroed) = (sem("c_" + n) for n in (
             "loaded", "turned_in", "sst_out", "last_set", "turned_out", "lastn_out", "stored", "mixed", "loras_in", "lora", "lora2",
             "lora_out", "lora_free", "norms_in", "norm_mm", "norm_rooted", "norm_rd", "rk_in", "rk_mm", "cums", "exps", "cdiff", "used",
             "chain", "act_chain", "zeroed"))
        tile_rows = [P] * 14 + [C_COLS - 14 * P]
        KC = W_MIX // P

        def vec(name):
            o = VOFF[name]
            return VT[:, o:o + 4].unsqueeze(2).broadcast_to([P, 4, TOK])

        def prompt_slots(buf, which):
            return (buf[:, :, 0:8, which, :] if which is not None else buf[:, :, 0:8, :])

        def sample_slots(buf, which):
            return (buf[:, :, 8:16, which, 0:DT] if which is not None else buf[:, :, 8:16, 0:DT])

        def prompt_of(t):
            return t[:, 0:4, 0:SEQ].rearrange("p i (c t) -> p i c t", t=CH)

        def samples_of(t):
            return t[:, 0:4, SEQ:TOK].rearrange("p i (c t) -> p i c t", t=DT)

        with nc.Block() as block:
            @block.sync
            def _(sp):
                sp.dma_start(SSN[:], io["state_shift"]).then_inc(loaded, 16)
                sp.dma_start(WUP[0:64, :], io["w_up"]).then_inc(loaded, 16)
                sp.dma_start(WUP[64:P, :], io["a_up"]).then_inc(loaded, 16)
                sp.dma_start(GUP[:, 0, :], io["g_up"][0:P, :]).then_inc(loaded, 16)
                sp.dma_start(GUP[0:32, 1, :], io["g_up"][P:160, :]).then_inc(loaded, 16)
                sp.dma_start(BO[:], io["head_ones"]).then_inc(loaded, 16)
                sp.dma_start(RESET[:], io["scan_reset"]).then_inc(loaded, 16)
                sp.wait_ge(lastn_out, 4)
                sp.dma_start(io["shift_prompt"], LASTN[0:1, :]).then_inc(stored, 16)
                sp.dma_start(io["shift_sample"], LASTN[1:NC_, :]).then_inc(stored, 16)
                sp.wait_ge(stored, 32)

            @block.gpsimd
            def _(gp):
                gp.memset(SST[:], 0.0).then_inc(zeroed, 1)
                gp.memset(AR[:], 0.0).then_inc(zeroed, 1)
                gp.memset(BK[:], 0.0).then_inc(zeroed, 1)
                gp.memset(VS[:], 0.0).then_inc(zeroed, 1)

            @block.tensor
            def _(pe):
                pe.wait_ge(loaded, 112)
                for i, n in enumerate(tile_rows):
                    mm = pe.transpose(PS[0:n, 0, i * NB:(i + 1) * NB], SSN[:, i * P:i * P + n], ident[0:NB, 0:NB])
                mm.then_inc(turned_in, 1)
                pe.wait_ge(last_set, 2)
                for i, n in enumerate(tile_rows):
                    mm = pe.transpose(PS[0:NC_, 1 + i // 4, i % 4 * P:i % 4 * P + n], LAST[0:n, i, :], ident[0:n, 0:n])
                mm.then_inc(turned_out, 1)
                pe.wait_ge(sst_out, 1)
                pe.wait_ge(lastn_out, 4)
                pe.wait_ge(loras_in, 2)
                for i in range(KC):
                    pe.matmul(PS[:, i, 0:TOK], WUP[0:64, i * P:(i + 1) * P], SG[0:64, 0, :], start=True, stop=True)
                    mm = pe.matmul(PS[:, 4 + i, 0:TOK], WUP[64:P, i * P:(i + 1) * P], PREV[64:P, 12, :], start=True, stop=True)
                mm.then_inc(lora, 1)
                pe.wait_ge(lora_out, 8)
                for i in range(KC):
                    pe.matmul(PS[:, i, 0:TOK], GUP[:, 0, i * P:(i + 1) * P], SG[:, 1, :], start=True, stop=False)
                    mm = pe.matmul(PS[:, i, 0:TOK], GUP[0:32, 1, i * P:(i + 1) * P], SG[0:32, 2, :], start=False, stop=True)
                mm.then_inc(lora2, 1)
                pe.wait_ge(norms_in, 1)
                for i in range(KC):
                    mm = pe.matmul(PS[:, 4 + i, 0:TOK], BO[:], T4[:, i, :], start=True, stop=True)
                mm.then_inc(norm_mm, 1)
                pe.wait_ge(lora_free, 1)
                pe.wait_ge(rk_in, 1)
                for i in range(KC):
                    mm = pe.matmul(PS[:, i, 0:TOK], BO[:], T5[:, i, :], start=True, stop=True)
                mm.then_inc(rk_mm, 1)

            @block.scalar
            def _(act):
                act.wait_ge(mixed, 1)
                act.activation(SG[0:64, 0, :], PREV[0:64, 12, :], ACT.Tanh).then_inc(loras_in, 1)
                act.activation(SG[:, 1:3, :], PREV[:, 13:15, :], ACT.Sigmoid).then_inc(loras_in, 1)
                act.wait_ge(lora, 1)
                for i in range(KC):
                    act.activation(LD[:, i, :], PS[:, i, 0:TOK], ACT.Sigmoid, bias=VT[:, VOFF["w0"] + i:VOFF["w0"] + i + 1]).then_inc(lora_out, 1)
                    act.activation(AA[:, i, :], PS[:, 4 + i, 0:TOK], ACT.Sigmoid, bias=VT[:, VOFF["a0"] + i:VOFF["a0"] + i + 1]).then_inc(lora_out, 1)
                act.wait_ge(lora2, 1)
                act.activation(G[:], PS[:, 0:4, 0:TOK], ACT.Copy).then_inc(lora_free, 1)
                act.wait_ge(norm_mm, 1)
                act.activation(T4[:], PS[:, 4:8, 0:TOK], ACT.Sqrt).then_inc(norm_rooted, 1)
                act.wait_ge(cdiff, 1)
                act.activation(T5[:], T5[:], ACT.Exp).then_inc(exps, 1)
                act.activation(PC[:, 0:4, :], PC[:, 8:12, :], ACT.Exp).then_inc(exps, 1)
                act.activation(PC[:, 4:8, :], PC[:, 8:12, :], ACT.Exp, scale=-1.0).then_inc(exps, 1)

            @block.vector
            def _(dve):
                chain = Chain(dve, chain_sem)
                dve.tensor_copy(LAST[:, :, 0:1], PC[:, :, SEQ - 1:SEQ]).then_inc(last_set, 1)
                dve.tensor_copy(LAST[:, :, 1:NC_], PC[:, :, SEQ + DT - 1:TOK:DT]).then_inc(last_set, 1)
                dve.memset(PREV[:, :, 0:1], 0.0)
                dve.tensor_copy(PREV[:, :, 1:TOK], PC[:, :, 0:TOK - 1])
                dve.wait_ge(zeroed, 4)
                dve.wait_ge(turned_in, 1)
                dve.tensor_copy(SST[:, 0:14, :], PS[:, 0, 0:14 * NB].rearrange("p (i b) -> p i b", b=NB))
                chain.link(dve.tensor_copy(SST[0:32, 14, :], PS[0:32, 0, 14 * NB:15 * NB]))
                chain.link(dve.tensor_copy(PREV[:, :, SEQ:TOK:DT], SST[:]))
                dve.sem_inc(sst_out, 1)
                dve.wait_ge(turned_out, 1)
                for j in range(4):
                    width = min(512, C_COLS - 512 * j)
                    dve.tensor_copy(LASTN[:, 512 * j:512 * j + width], PS[0:NC_, 1 + j, 0:width]).then_inc(lastn_out, 1)
                mu = VT[:, VOFF["mu_shift"]:VOFF["mu_shift"] + 15].unsqueeze(2).broadcast_to([P, 15, TOK])
                chain.link(dve.tensor_tensor(PREV[:], PREV[:], PC[:], ALU.subtract))
                chain.link(dve.tensor_tensor(PREV[:], PREV[:], mu, ALU.mult))
                dve.tensor_tensor(PREV[:], PREV[:], PC[:], ALU.add).then_inc(mixed, 1)
                dve.wait_ge(mixed, 1)
                r, k, v = PREV[:, 0:4, :], PREV[:, 4:8, :], PREV[:, 8:12, :]
                chain.link(dve.tensor_tensor(KK[:], k, vec("k_k"), ALU.mult))
                dve.tensor_tensor(T4[:], KK[:], KK[:], ALU.mult).then_inc(norms_in, 1)
                dve.wait_ge(lora_out, 8)
                chain.link(dve.scalar_tensor_tensor(T5[:], AA[:], -1.0, vec("k_a"), ALU.add, ALU.mult))
                chain.link(dve.scalar_tensor_tensor(k, T5[:], 1.0, k, ALU.add, ALU.mult))
                chain.link(dve.tensor_tensor(T5[:], r, k, ALU.mult))
                dve.tensor_tensor(T5[:], T5[:], vec("r_k"), ALU.mult).then_inc(rk_in, 1)
                chain.link(dve.tensor_scalar(LD[:], LD[:], LOG_DECAY, None, ALU.mult))
                for i in range(KC):
                    last = dve.tensor_tensor_scan(PC[:, 8 + i, :], RESET[:], LD[:, i, :], 0.0, ALU.mult, ALU.add)
                chain.link(last)
                dve.wait_ge(norm_rooted, 1)
                chain.link(dve.tensor_scalar(T4[:], T4[:], 1e-12, None, ALU.max))
                chain.link(dve.reciprocal(T4[:], T4[:]))
                chain.link(dve.tensor_tensor(KK[:], KK[:], T4[:], ALU.mult))
                dve.wait_ge(rk_mm, 1)
                dve.tensor_tensor(BON[:], PS[:, 0:4, 0:TOK], v, ALU.mult)
                dve.tensor_tensor(T5[:], PC[:, 8:12, :], LD[:], ALU.subtract).then_inc(cdiff, 1)
                dve.tensor_tensor(AA[:], AA[:], KK[:], ALU.mult)
                chain.link(dve.tensor_scalar(KK[:], KK[:], -1.0, None, ALU.mult))
                dve.tensor_copy(prompt_slots(VS, None), prompt_of(v))
                dve.tensor_copy(sample_slots(VS, None), samples_of(v))
                dve.wait_ge(exps, 3)
                up, inv = PC[:, 0:4, :], PC[:, 4:8, :]
                for buf, which, x, y in ((AR, 0, KK, T5), (AR, 1, r, up), (BK, 0, AA, inv), (BK, 1, k, inv)):
                    dve.tensor_tensor(prompt_slots(buf, which), prompt_of(x), prompt_of(y), ALU.mult)
                    dve.tensor_tensor(sample_slots(buf, which), samples_of(x), samples_of(y), ALU.mult)
                dve.tensor_copy(PEND[:, :, 0:8], PC[:, 0:4, CH - 1:SEQ:CH])
                dve.tensor_copy(PEND[:, :, 8:16], PC[:, 0:4, SEQ + DT - 1:TOK:DT])

    def rwkv_chunks_phase(AR, BK, VS, PEND, YT):
        NQ = NCH * NH
        UU = sb("UU", [CH, NQ, CH])
        UB, WB_, TB = sb("UB", [NQ, CH, CH]), sb("WBl", [NQ, CH, CH]), sb("TB", [NQ, CH * CH])
        GM = sb("GM", [64, 64])
        SN, SO = sb("SN", [P, NB, 4, HD]), sb("SO", [P, 1 + NB, 4, HD])
        ST = sb("ST_c", [P, 1 + NB, 4, HD])
        GE, BKN, VV, RH = (sb("GE", [64, 2, NH, 64]), sb("BKN", [64, 2, 512]), sb("VV", [64, 2, 512]), sb("RH", [CH, 2, 512]))
        scratch_u, scratch_w = (nc.dram_tensor(n, (NQ, CH, CH), F32).ap() for n in ("scratch_u", "scratch_w"))
        loaded, sn_turned, st_set, m_done, m_out, moved, solved, chain_sem = (sem("x_" + n) for n in (
            "loaded", "sn_turned", "st_set", "m_done", "m_out", "moved", "solved", "chain"))
        ga, ev_a, rb, mv_out, ev_b, sc, ev_c, yd, ev_s, ev_y = ([sem(f"x_{n}{u}") for u in range(2)] for n in (
            "ga", "ev_a", "rb", "mv_out", "ev_b", "sc", "ev_c", "yd", "ev_s", "ev_y"))
        so_turned, so_out, stored = sem("x_so_turned"), sem("x_so_out"), sem("x_stored")
        STEPS = NCH // 2

        def lo(h):
            return slice(64 * (h % 2), 64 * (h % 2) + 64)

        with nc.Block() as block:
            @block.sync
            def _(sp):
                for b in range(NB):
                    sp.dma_start(SN[:, b], io["state_rwkv"][b].rearrange("(i g) v k -> (g v) i k", g=2)).then_inc(loaded, 16)
                sp.dma_start(GM[:], io["chunk_mask"]).then_inc(loaded, 16)
                sp.wait_ge(m_out, 8)
                sp.dma_start(scratch_u.rearrange("q s t -> s q t"), UU[:]).then_inc(moved, 16)
                sp.wait_ge(moved, 16)
                sp.dma_start(UB[:], scratch_u).then_inc(moved, 16)
                sp.wait_ge(solved, 1)
                sp.dma_start(scratch_w, WB_[:]).then_inc(moved, 16)
                sp.wait_ge(moved, 48)
                sp.dma_start(UU[:], scratch_w.rearrange("q s t -> s q t")).then_inc(moved, 16)
                sp.wait_ge(so_out, 5)
                sp.dma_start(io["rwkv_prompt"].rearrange("o (i g) v k -> (g v) (o i) k", g=2), SO[:, 0]).then_inc(stored, 16)
                sp.dma_start(io["rwkv_sample"].rearrange("b (i g) v k -> (g v) b i k", g=2), SO[:, 1:]).then_inc(stored, 16)
                sp.wait_ge(stored, 32)

            @block.tensor
            def _(pe):
                pe.wait_ge(loaded, 16 * NB + 16)
                for n in range(8):
                    for j in range(16):
                        c, h = 4 * (n % 4) + j // 4, 2 * (j % 4) + n // 4
                        mm = pe.matmul(PS[0:CH, n, j * CH:(j + 1) * CH], BK[lo(h), h // 2, c, 0, :], AR[lo(h), h // 2, c, 0, :], start=True, stop=True)
                    mm.then_inc(m_done, 1)
                pe.wait_ge(m_out, 8)
                for b in range(NB):
                    for h in range(NH):
                        c = (b % 2) * 256 + h // 2 * HD
                        mm = pe.matmul(PS[lo(h), b // 2, c:c + HD], SN[lo(h), b, h // 2, :], ident[lo(h), lo(h)], start=True, stop=True)
                mm.then_inc(sn_turned, 1)

                def chunk_a(s, u):
                    c = s + 8 * u
                    if s >= 1:
                        pe.wait_ge(ev_s[u], 3 * s)
                        pe.wait_ge(ev_y[u], s)
                    for h in range(NH):
                        pe.matmul(PS[0:64, 4 * u + h % 2, h // 2 * 64:(h // 2 + 1) * 64], BK[lo(h), h // 2, c].rearrange("p a t -> p (a t)"),
                                  AR[lo(h), h // 2, c].rearrange("p a t -> p (a t)"), start=True, stop=True)
                    for i in range(4):
                        pe.transpose(PS[0:64, 4 * u + 2, i * P:(i + 1) * P], BK[:, i, c].rearrange("p a t -> p (a t)"), ident[:])
                    for i in range(4):
                        mm = pe.matmul(PS[CH:2 * CH, 4 * u + 3, i * P:(i + 1) * P], VS[:, i, c, :], ident[:], start=True, stop=True)
                    mm.then_inc(ga[u], 1)

                def chunk_b(s, u):
                    c = s + 8 * u
                    st = 1 + s if u else 0
                    pe.wait_ge(ev_a[u], 4 * (s + 1))
                    for h in range(NH):
                        pe.matmul(PS[0:CH, 4 * u + 3, h * 64:(h + 1) * 64], GE[CH:2 * CH, u, h, 0:CH], VV[CH:2 * CH, u, h * 64:(h + 1) * 64],
                                  start=True, stop=True)
                    for h in range(NH):
                        mm = pe.matmul(PS[0:CH, 4 * u + h % 2, h // 2 * 64:(h // 2 + 1) * 64], AR[lo(h), h // 2, c, 0, :],
                                       ST[lo(h), st, h // 2, :], start=True, stop=True)
                    mm.then_inc(rb[u], 1)

                def chunk_c(s, u):
                    c = s + 8 * u
                    pe.wait_ge(ev_b[u], 2 * (s + 1))
                    for h in range(NH):
                        mm = pe.matmul(PS[0:CH, 4 * u + 2, h * 64:(h + 1) * 64], UU[:, c * NH + h, :], RH[:, u, h * 64:(h + 1) * 64], start=True, stop=True)
                    mm.then_inc(sc[u], 1)

                def chunk_d(s, u):
                    c = s + 8 * u
                    st = 1 + s if u else 0
                    pe.wait_ge(ev_c[u], s + 1)
                    for h in range(NH):
                        i = h // 2
                        new = VV[:, u, h * 64:(h + 1) * 64]
                        pe.matmul(PS[lo(h), 4 * u, i * CH:(i + 1) * CH], ST[lo(h), st, i, :], AR[lo(h), i, c, 1, :], start=True, stop=True)
                        pe.matmul(PS[lo(h), 4 * u + 3, 256 + i * CH:256 + (i + 1) * CH], new, GE[:, u, h, CH:2 * CH], start=True, stop=True)
                        mm = pe.matmul(PS[lo(h), 4 * u + 3, i * HD:(i + 1) * HD], BKN[:, u, h * 64:(h + 1) * 64], new, start=True, stop=True)
                    mm.then_inc(yd[u], 1)

                pe.wait_ge(st_set, 5)
                pe.wait_ge(moved, 64)
                for s in range(STEPS):
                    for stage_of in (chunk_a, chunk_b, chunk_c, chunk_d):
                        for u in range(2):
                            stage_of(s, u)
                for u in range(2):
                    pe.wait_ge(ev_s[u], 3 * STEPS)
                    pe.wait_ge(ev_y[u], STEPS)
                for b in range(1 + NB):
                    for h in range(NH):
                        c = (b % 2) * 256 + h // 2 * HD
                        mm = pe.matmul(PS[lo(h), b // 2, c:c + HD], ST[lo(h), b, h // 2, :], ident[lo(h), lo(h)], start=True, stop=True)
                mm.then_inc(so_turned, 1)

            @block.scalar
            def _(act):
                for s in range(STEPS):
                    for u in range(2):
                        act.wait_ge(rb[u], s + 1)
                        act.activation(RH[:, u, :], PS[0:CH, 4 * u + 3, :], ACT.Copy).then_inc(mv_out[u], 1)
                    for u in range(2):
                        act.wait_ge(sc[u], s + 1)
                        act.activation(VV[0:CH, u, :], PS[0:CH, 4 * u + 2, :], ACT.Copy).then_inc(ev_c[u], 1)
                    for u in range(2):
                        act.wait_ge(yd[u], s + 1)
                        n, t0 = (DT, SEQ + DT * s) if u else (CH, CH * s)
                        act.activation(YT[:, :, t0:t0 + n], PS[:, 4 * u, 0:4 * CH].rearrange("p (i t) -> p i t", t=CH)[:, :, 0:n],
                                       ACT.Copy).then_inc(ev_y[u], 1)

            @block.vector
            def _(dve):
                chain = Chain(dve, chain_sem)
                dve.wait_ge(loaded, 16 * NB + 16)
                for n in range(8):
                    dve.wait_ge(m_done, n + 1)
                    blocks = UU[:].rearrange("p (n j g) t -> p n g j t", n=4, g=2)[:, n % 4, n // 4]
                    dve.tensor_tensor(blocks, PS[0:CH, n, :].rearrange("p (j t) -> p j t", t=CH),
                                      GM[0:CH, 0:CH].unsqueeze(1).broadcast_to([CH, 16, CH]), ALU.mult).then_inc(m_out, 1)
                dve.memset(ST[:, 0], 0.0).then_inc(st_set, 1)
                dve.wait_ge(sn_turned, 1)
                for n in range(4):
                    dve.tensor_copy(ST[:, 1 + 2 * n:3 + 2 * n], PS[:, n, :].rearrange("p (b i k) -> p b i k", b=2, i=4)).then_inc(st_set, 1)
                flat = WB_[:].rearrange("q s t -> q (s t)")
                chain.link(dve.memset(WB_[:], 0.0))
                chain.link(dve.memset(flat[:, 0:CH * CH:CH + 1], 1.0))
                dve.wait_ge(moved, 32)
                for s in range(CH - 2, -1, -1):
                    n = CH - 1 - s
                    tmp = TB[:, 0:n * n].rearrange("q (t j) -> q t j", j=n)
                    chain.link(dve.tensor_tensor(tmp, WB_[:, s + 1:CH, s + 1:CH].rearrange("q j t -> q t j"),
                                                 UB[:, s, s + 1:CH].unsqueeze(1).broadcast_to([NQ, n, n]), ALU.mult))
                    last = dve.tensor_reduce(WB_[:, s, s + 1:CH], tmp, AX.X, ALU.add)
                    if s:
                        chain.link(last)
                last.then_inc(solved, 1)
                for s in range(STEPS):
                    for u in range(2):
                        dve.wait_ge(ga[u], s + 1)
                        for g in range(2):
                            dve.tensor_tensor(GE[:, u].rearrange("p (i g) t -> p g i t", g=2)[:, g],
                                              PS[0:64, 4 * u + g, 0:256].rearrange("p (i t) -> p i t", t=64),
                                              GM[:].unsqueeze(1).broadcast_to([64, 4, 64]), ALU.mult).then_inc(ev_a[u], 1)
                        dve.tensor_copy(BKN[:, u, :], PS[0:64, 4 * u + 2, :]).then_inc(ev_a[u], 1)
                        dve.tensor_copy(VV[CH:2 * CH, u, :], PS[CH:2 * CH, 4 * u + 3, :]).then_inc(ev_a[u], 1)
                    for u in range(2):
                        dve.wait_ge(mv_out[u], s + 1)
                        for g in range(2):
                            rows = RH[:, u].rearrange("p (i g v) -> p g i v", g=2, v=HD)[:, g]
                            dve.tensor_tensor(rows, rows, PS[0:CH, 4 * u + g, 0:256].rearrange("p (i v) -> p i v", v=HD), ALU.add).then_inc(ev_b[u], 1)
                    for u in range(2):
                        st = 1 + s if u else 0
                        dve.wait_ge(yd[u], s + 1)
                        dve.tensor_tensor(ST[:, st], PS[:, 4 * u + 3, 0:256].rearrange("p (i v) -> p i v", v=HD), ST[:, st], ALU.add).then_inc(ev_s[u], 1)
                        dve.wait_ge(ev_s[u], 3 * s + 1)
                        dve.tensor_tensor(ST[:, st], ST[:, st], PEND[:, :, s + 8 * u].unsqueeze(2).broadcast_to([P, 4, HD]), ALU.mult).then_inc(ev_s[u], 1)
                        n, t0 = (DT, SEQ + DT * s) if u else (CH, CH * s)
                        dve.wait_ge(ev_y[u], s + 1)
                        dve.tensor_tensor(YT[:, :, t0:t0 + n], YT[:, :, t0:t0 + n],
                                          PS[:, 4 * u + 3, 256:256 + 4 * CH].rearrange("p (i t) -> p i t", t=CH)[:, :, 0:n], ALU.add).then_inc(ev_s[u], 1)
                dve.wait_ge(so_turned, 1)
                for n in range(5):
                    k = 2 if n < 4 else 1
                    dve.tensor_copy(SO[:, 2 * n:2 * n + k], PS[:, n, 0:256 * k].rearrange("p (b i k) -> p b i k", b=k, i=4)).then_inc(so_out, 1)

    def rwkv_output_phase(YT, G, BON, Y):
        BO, SQ = sb("BO2", [P, P]), sb("SQ_c", [P, 4, TOK])
        loaded, mean_mm, centred, var_mm, rs, rooted, chain_sem = (sem("g_" + n) for n in (
            "loaded", "mean_mm", "centred", "var_mm", "rs", "rooted", "chain"))

        def vec(name):
            o = VOFF[name]
            return VT[:, o:o + 4].unsqueeze(2).broadcast_to([P, 4, TOK])

        with nc.Block() as block:
            @block.sync
            def _(sp):
                sp.dma_start(BO[:], io["head_ones"]).then_inc(loaded, 16)

            @block.tensor
            def _(pe):
                pe.wait_ge(loaded, 16)
                for i in range(4):
                    mm = pe.matmul(PS[:, i, 0:TOK], BO[:], YT[:, i, :], start=True, stop=True)
                mm.then_inc(mean_mm, 1)
                pe.wait_ge(centred, 1)
                for i in range(4):
                    mm = pe.matmul(PS[:, 4 + i, 0:TOK], BO[:], SQ[:, i, :], start=True, stop=True)
                mm.then_inc(var_mm, 1)

            @block.scalar
            def _(act):
                act.wait_ge(rs, 1)
                act.activation(SQ[:], SQ[:], ACT.Sqrt).then_inc(rooted, 1)

            @block.vector
            def _(dve):
                chain = Chain(dve, chain_sem)
                dve.wait_ge(mean_mm, 1)
                chain.link(dve.tensor_scalar(SQ[:], PS[:, 0:4, 0:TOK], 1.0 / HD, None, ALU.mult))
                chain.link(dve.tensor_tensor(YT[:], YT[:], SQ[:], ALU.subtract))
                dve.tensor_tensor(SQ[:], YT[:], YT[:], ALU.mult).then_inc(centred, 1)
                dve.wait_ge(var_mm, 1)
                dve.tensor_scalar(SQ[:], PS[:, 4:8, 0:TOK], 1.0 / HD, GN_EPS, ALU.mult, ALU.add).then_inc(rs, 1)
                dve.wait_ge(rooted, 1)
                chain.link(dve.reciprocal(SQ[:], SQ[:]))
                chain.link(dve.tensor_tensor(YT[:], YT[:], SQ[:], ALU.mult))
                chain.link(dve.tensor_tensor(YT[:], YT[:], vec("lnx_w"), ALU.mult))
                chain.link(dve.tensor_tensor(YT[:], YT[:], vec("lnx_b"), ALU.add))
                chain.link(dve.tensor_tensor(YT[:], YT[:], BON[:], ALU.add))
                chain.link(dve.tensor_tensor(Y[:, 0:4, :], YT[:], G[:], ALU.mult))

    def store_phase():
        YN = sb("YN", [P, 3, D])
        turned, copied, stored = sem("y_turned"), sem("y_copied"), sem("y_stored")
        units = [(t, j) for t in range(3) for j in range(2)]
        with nc.Block() as block:
            @block.tensor
            def _(pe):
                for u, (t, j) in enumerate(units):
                    n = P if t < 2 else NS
                    for i in range(4):
                        mm = pe.transpose(PS[0:n, u, i * P:(i + 1) * P], H[:, 4 * j + i, t * P:t * P + n], ident[:])
                    mm.then_inc(turned, 1)

            @block.vector
            def _(dve):
                for u, (t, j) in enumerate(units):
                    n = P if t < 2 else NS
                    dve.wait_ge(turned, u + 1)
                    dve.tensor_copy(YN[0:n, t, j * 512:(j + 1) * 512], PS[0:n, u, :]).then_inc(copied, 1)

            @block.sync
            def _(sp):
                for t in range(3):
                    sp.wait_ge(copied, 2 * (t + 1))
                    if t < 2:
                        sp.dma_start(io["y_prompt"][0, t * P:(t + 1) * P, :], YN[:, t, :]).then_inc(stored, 16)
                    else:
                        sp.dma_start(io["y_sample"].rearrange("b t d -> (b t) d"), YN[0:NS, t, :]).then_inc(stored, 16)
                sp.wait_ge(stored, 48)

    def router_phase(GB, PB, POS, HN, ITEMS):
        RW, SEL = sb("RW", [P, KT, NE]), sb("SEL", [NE, NE, P])
        TIE2, BEFORE = sb("TIE2", [P, 64]), sb("BEFORE", [P, P])
        LG, GT, PT = sb("LG", [P, 3, NE]), sb("r_GT", [NE, TOK]), sb("r_PT", [NE, TOK])
        G1, G2 = sb("rG1", [P, 3, 8, 8]), sb("rG2", [P, 3, 8, 8])
        MK, top, den = sb("r_mask", [P, 3, NE]), sb("r_top", [P, 3]), sb("r_den", [P, 3])
        FL, FS, FB = sb("r_flags", [1, 2 * NE]), sb("r_flags_sum", [1, 2 * NE]), sb("r_before", [1, 2 * NE])
        PICK, FOUND, ITAB = sb("r_pick", [1, 3, MORE, 2 * NE]), sb("r_found", [1, 2, MORE]), sb("r_item_table", [1, 3, MORE, 2 * NE])
        loaded, logits, shifted, exped, turn_in, turned, gt_out, spread, chain_sem = (sem("r_" + n) for n in (
            "loaded", "logits", "shifted", "exped", "turn_in", "turned", "gt_out", "spread", "chain"))
        filled, masked, counted, hn_turned, hn_out = (sem("r_" + n) for n in ("filled", "masked", "counted", "hn_turned", "hn_out"))
        with nc.Block() as block:
            @block.sync
            def _(sp):
                sp.dma_start(RW[:], io["router_w"].rearrange("(k p) e -> p k e", p=P)).then_inc(loaded, 16)
                sp.dma_start(SEL[:], io["expert_select"]).then_inc(loaded, 16)
                sp.dma_start(TIE2[:], io["tie"]).then_inc(loaded, 16)
                sp.dma_start(BEFORE[:], io["before"]).then_inc(loaded, 16)
                sp.dma_start(ITAB[:], io["item_table"]).then_inc(loaded, 16)

            @block.tensor
            def _(pe):
                pe.wait_ge(loaded, 80)
                for t in range(3):
                    n = P if t < 2 else NS
                    for k in range(KT):
                        mm = pe.matmul(PS[0:n, 0, t * NE:(t + 1) * NE], H[:, k, t * P:t * P + n], RW[:, k, :], start=(k == 0), stop=(k == KT - 1))
                mm.then_inc(logits, 1)
                for u in range(6):
                    t, half = u // 2, u % 2
                    n = P if t < 2 else NS
                    if u >= 2:
                        pe.wait_ge(hn_out, u - 1)
                    for i in range(4):
                        mm = pe.transpose(PS[0:n, 6 + half, i * P:(i + 1) * P], H[:, 4 * half + i, t * P:t * P + n], ident[:])
                    mm.then_inc(hn_turned, 1)
                pe.wait_ge(masked, 1)
                for t in range(3):
                    out = PS[:, 1, t * NE:(t + 1) * NE]
                    pe.matmul(out, BEFORE[:], MK[:, t, :], start=True, stop=(t == 0))
                    for a in range(t):
                        pe.matmul(out, ones[:], MK[:, a, :], start=False, stop=(a == t - 1))
                for t in range(3):
                    mm = pe.matmul(PS[:, 1, 3 * NE:4 * NE], ones[:], MK[:, t, :], start=(t == 0), stop=(t == 2))
                mm.then_inc(counted, 1)
                pe.wait_ge(turn_in, 2)
                for t in range(3):
                    n = P if t < 2 else NS
                    pe.transpose(PS[0:NE, 2, t * P:t * P + n], LG[0:n, t, :], ident[0:n, 0:n])
                    mm = pe.transpose(PS[0:NE, 3, t * P:t * P + n], POS[0:n, t, :], ident[0:n, 0:n])
                mm.then_inc(turned, 1)
                pe.wait_ge(gt_out, 2)
                pe.wait_ge(hn_out, 6)
                for j in range(2 * NE):
                    if j >= 4:
                        pe.wait_ge(spread, j - 3)
                    pe.matmul(PS[:, 4 + j % 4, 0:TOK], SEL[:, j // 2, :], (GT, PT)[j % 2][:], start=True, stop=True).then_inc(filled, 1)

            @block.scalar
            def _(act):
                for u in range(6):
                    t, half = u // 2, u % 2
                    n = P if t < 2 else NS
                    act.wait_ge(hn_turned, u + 1)
                    act.activation(HN[0:n, t, half * 512:(half + 1) * 512], PS[0:n, 6 + half, :], ACT.Copy).then_inc(hn_out, 1)
                act.wait_ge(shifted, 1)
                act.activation(LG[:], LG[:], ACT.Exp).then_inc(exped, 1)

            @block.vector
            def _(dve):
                chain = Chain(dve, chain_sem)
                chain.link(dve.memset(LG[:], 0.0))
                dve.wait_ge(loaded, 80)
                dve.wait_ge(logits, 1)
                dve.tensor_copy(LG[:, 0:2, :], PS[:, 0, 0:2 * NE].rearrange("p (t e) -> p t e", e=NE))
                chain.link(dve.tensor_copy(LG[0:NS, 2, :], PS[0:NS, 0, 2 * NE:3 * NE]))
                for t in range(3):
                    theirs, own = LG[:, t, :].unsqueeze(1).broadcast_to([P, 8, 8]), LG[:, t, :].unsqueeze(2).broadcast_to([P, 8, 8])
                    dve.tensor_tensor(G1[:, t], theirs, own, ALU.is_gt)
                    last = dve.tensor_tensor(G2[:, t], theirs, own, ALU.is_equal)
                chain.link(last)
                chain.link(dve.tensor_tensor(G2[:].rearrange("p t i j -> p t (i j)"), G2[:].rearrange("p t i j -> p t (i j)"),
                                             TIE2[:].unsqueeze(1).broadcast_to([P, 3, 64]), ALU.mult))
                chain.link(dve.tensor_tensor(G1[:], G1[:], G2[:], ALU.add))
                dve.tensor_reduce(MK[:], G1[:], AX.X, ALU.add)
                chain.link(dve.tensor_reduce(top[:], LG[:], AX.X, ALU.max))
                chain.link(dve.tensor_scalar(MK[:], MK[:], 1.5, None, ALU.is_lt))
                dve.memset(MK[NS:P, 2, :], 0.0).then_inc(masked, 1)
                dve.tensor_tensor(LG[:], LG[:], top[:].unsqueeze(2).broadcast_to([P, 3, NE]), ALU.subtract).then_inc(shifted, 1)
                dve.wait_ge(masked, 1)
                chain.link(dve.tensor_scalar(POS[:], MK[:], -1000.0, 1000.0, ALU.mult, ALU.add))
                dve.wait_ge(counted, 1)
                dve.tensor_tensor(POS[:], POS[:], PS[:, 1, 0:3 * NE].rearrange("p (t e) -> p t e", e=NE), ALU.add).then_inc(turn_in, 1)
                for c in range(2):
                    last = dve.tensor_scalar(FL[:, c * NE:(c + 1) * NE], PS[0:1, 1, 3 * NE:4 * NE], (c + 1) * P + 0.5, None, ALU.is_gt)
                chain.link(last)
                chain.link(dve.tensor_tensor_scan(FS[:], ones[0:1, 0:2 * NE], FL[:], 0.0, ALU.mult, ALU.add))
                chain.link(dve.tensor_tensor(FB[:], FS[:], FL[:], ALU.subtract))
                many = [1, MORE, 2 * NE]
                chain.link(dve.tensor_tensor(PICK[:, 0], FB[:].unsqueeze(1).broadcast_to(many), ITAB[:, 0], ALU.is_equal))
                chain.link(dve.tensor_tensor(PICK[:, 0], PICK[:, 0], FL[:].unsqueeze(1).broadcast_to(many), ALU.mult))
                for j in range(2):
                    last = dve.tensor_tensor(PICK[:, 1 + j], PICK[:, 0], ITAB[:, 1 + j], ALU.mult)
                chain.link(last)
                chain.link(dve.tensor_reduce(FOUND[:], PICK[:, 1:3], AX.X, ALU.add))
                for j in range(2):
                    dve.tensor_copy(ITEMS[:, j * (NE + MORE) + NE:(j + 1) * (NE + MORE)], FOUND[:, j, :])
                dve.tensor_copy(ITEMS[:, 2 * (NE + MORE):], FS[:, 2 * NE - 1:2 * NE])
                dve.tensor_copy(ITEMS[:, 0:NE], ITAB[:, 1, 0, 0:NE])
                dve.tensor_scalar(ITEMS[:, NE + MORE:NE + MORE + NE], ITAB[:, 1, 0, 0:NE], 0.0, None, ALU.mult)
                dve.wait_ge(exped, 1)
                chain.link(dve.tensor_tensor(LG[:], LG[:], MK[:], ALU.mult))
                chain.link(dve.tensor_reduce(den[:, 0:2], LG[:, 0:2, :], AX.X, ALU.add))
                chain.link(dve.tensor_reduce(den[0:NS, 2:3], LG[0:NS, 2:3, :], AX.X, ALU.add))
                chain.link(dve.memset(den[NS:P, 2:3], 1.0))
                chain.link(dve.reciprocal(den[:], den[:]))
                dve.tensor_tensor(LG[:], LG[:], den[:].unsqueeze(2).broadcast_to([P, 3, NE]), ALU.mult).then_inc(turn_in, 1)
                dve.wait_ge(turned, 1)
                dve.tensor_copy(GT[:], PS[0:NE, 2, 0:TOK]).then_inc(gt_out, 1)
                dve.tensor_copy(PT[:], PS[0:NE, 3, 0:TOK]).then_inc(gt_out, 1)
                for j in range(2 * NE):
                    dve.wait_ge(filled, j + 1)
                    dve.tensor_copy((GB, PB)[j % 2][:, j // 2, :], PS[:, 4 + j % 4, 0:TOK]).then_inc(spread, 1)

    def experts_phase(GB, PB, POS, HN, ITEMS):
        R = 6
        RING = sb("moe_ring", [P, R, KT, 512])
        HID, HT = sb("moe_hid", [P, 2, 512]), sb("moe_HT", [P, FT, P])
        XE, YE = sb("moe_XE", [P, KT, P]), sb("moe_YE", [P, D])
        SL, GT = sb("moe_SL", [P, 3, P]), sb("moe_GT", [P, TOK])
        IOTA, IOTAP = sb("moe_iota", [P, 3, P]), sb("moe_iota_p", [P, 3])
        tmp = sb("moe_tmp", [P, NS])
        panel_in = [sem(f"moe_in{i}") for i in range(R)]
        (tables, sel_set, gathered, xe_out, up_done, silu_done, hid_done, hid_turned, ht_out, down_done, y_out, gt_set, scattered,
         added, chain_sem) = (sem("moe_" + n) for n in (
             "tables", "sel_set", "gathered", "xe_out", "up_done", "silu_done", "hid_done", "hid_turned", "ht_out", "down_done", "y_out",
             "gt_set", "scattered", "added", "chain"))
        CHUNKS = [(c, min(512, DFF - c)) for c in range(0, DFF, 512)]
        NC6 = len(CHUNKS)
        DOWN = [(half, k, min(8, FT - k)) for half in range(2) for k in range(0, FT, 8)]
        NPAN = 2 * NC6 + len(DOWN)
        assert NPAN % R == 0 and NC6 == len(DOWN) == 6

        def ge(eng, semaphore, per, e, k):
            if isinstance(e, int):
                if per * e + k > 0:
                    eng.wait_ge(semaphore, per * e + k)
            else:
                eng.wait_ge(semaphore, e * per + k)

        def one(buf, n):
            return buf[:, n] if isinstance(n, int) else buf[:, bass.ds(n, 1)].rearrange("p o t -> p (o t)")

        def expert_of(eng, i):
            return i if isinstance(i, int) else eng.value_load(ITEMS[0:1, bass.ds(i, 1)], min_val=0, max_val=NE - 1)

        def chunk_of(eng, i):
            return 0 if isinstance(i, int) else eng.value_load(ITEMS[0:1, bass.ds(i + (NE + MORE), 1)], min_val=0, max_val=2)

        def loop(eng, body):
            more = eng.value_load(ITEMS[0:1, 2 * (NE + MORE):2 * (NE + MORE) + 1], min_val=0, max_val=MORE)
            body(0, True, False)
            with eng.Fori(1, more + (NE - 1)) as i:
                body(i, False, False)
            body(more + (NE - 1), False, True)
            return more + NE

        with nc.Block() as block:
            @block.sync
            def _(sp):
                sp.dma_start(IOTA[:], io["iota"]).then_inc(tables, 16)
                sp.dma_start(IOTAP[:], io["iota_p"]).then_inc(tables, 16)

                def body(e, first, last):
                    expert = expert_of(sp, e)

                    def weights(name):
                        w = io[name]
                        return w[expert] if isinstance(expert, int) else w[bass.ds(expert, 1)].rearrange("o k n -> (o k) n")
                    w1, w3, w2 = weights("moe_w1"), weights("moe_w3"), weights("moe_w2")
                    for n in range(NPAN):
                        back = n - R
                        if back < 0:
                            ge(sp, down_done, 6, e, back + 1)
                        elif back < 2 * NC6:
                            ge(sp, up_done, 6, e, back // 2 + 1)
                        else:
                            ge(sp, down_done, 6, e, back - 2 * NC6 + 1)
                        if n < 2 * NC6:
                            c, width = CHUNKS[n // 2]
                            src = (w1, w3)[n % 2][:, c:c + width].rearrange("(k p) n -> p k n", p=P)
                            sp.dma_start(RING[:, n % R, :, 0:width], src).then_inc(panel_in[n % R], 16)
                        else:
                            half, k, nk = DOWN[n - 2 * NC6]
                            src = w2[k * P:(k + nk) * P, half * 512:(half + 1) * 512].rearrange("(k p) n -> p k n", p=P)
                            sp.dma_start(RING[:, n % R, 0:nk, :], src).then_inc(panel_in[n % R], 16)
                loop(sp, body)

            @block.tensor
            def _(pe):
                def arrived(e, n):
                    ge(pe, panel_in[n % R], 16 * (NPAN // R), e, 16 * (n // R + 1))

                def gather(e):
                    ge(pe, sel_set, 1, e, 1)
                    ge(pe, hid_done, 6, e, -1)
                    for k in range(KT):
                        for t in range(3):
                            n = P if t < 2 else NS
                            mm = pe.matmul(PS[:, k // 4, k % 4 * P:(k % 4 + 1) * P], HN[0:n, t, k * P:(k + 1) * P], SL[0:n, t, :],
                                           start=(t == 0), stop=(t == 2))
                    mm.then_inc(gathered, 1)

                def up(e, c):
                    if c == 0:
                        ge(pe, xe_out, 2, e, 2)
                    arrived(e, 2 * c)
                    arrived(e, 2 * c + 1)
                    ge(pe, hid_done, 6, e, c - 1)
                    width = CHUNKS[c][1]
                    for w in range(2):
                        for k in range(KT):
                            mm = pe.matmul(PS[:, 2 * (c % 2) + w, 0:width], XE[:, k, :], RING[:, (2 * c + w) % R, k, 0:width],
                                           start=(k == 0), stop=(k == KT - 1))
                    mm.then_inc(up_done, 1)

                def turn(e, c):
                    ge(pe, hid_done, 6, e, c + 1)
                    ge(pe, ht_out, 6, e, c - 1)
                    if c < 2:
                        ge(pe, added, KT, e, 0)
                    for i in range(CHUNKS[c][1] // P):
                        mm = pe.transpose(PS[:, 4 + c % 2, i * P:(i + 1) * P], HID[:, c % 2, i * P:(i + 1) * P], ident[:])
                    mm.then_inc(hid_turned, 1)

                def down(e):
                    ge(pe, added, KT, e, 0)
                    for d, (half, k0, nk) in enumerate(DOWN):
                        arrived(e, 2 * NC6 + d)
                        ge(pe, ht_out, 6, e, (k0 + nk + 3) // 4)
                        for k in range(nk):
                            mm = pe.matmul(PS[:, 6 + half, :], HT[:, k0 + k, :], RING[:, (2 * NC6 + d) % R, k, :],
                                           start=(k0 + k == 0), stop=(k0 + k == FT - 1))
                        mm.then_inc(down_done, 1)

                def scatter(e, part):
                    ge(pe, gt_set, 1, e, 0)
                    ge(pe, y_out, 2, e, 0)
                    for k in range(4 * part, 4 * part + 4):
                        if k >= 4:
                            ge(pe, added, KT, e, k - 3 - KT)
                        if k < 2:
                            ge(pe, ht_out, 6, e, 0)
                        pe.matmul(PS[:, 4 + k % 4, 0:TOK], YE[:, k * P:(k + 1) * P], GT[:], start=True, stop=True).then_inc(scattered, 1)

                def body(e, first, last):
                    up(e, 0)
                    if not first:
                        scatter(e, 0)
                    up(e, 1)
                    if not first:
                        scatter(e, 1)
                    up(e, 2)
                    turn(e, 0)
                    for c in range(3, NC6):
                        turn(e, c - 2)
                        up(e, c)
                    if not last:
                        gather(e + 1)
                    turn(e, NC6 - 2)
                    turn(e, NC6 - 1)
                    down(e)

                gather(0)
                n = loop(pe, body)
                scatter(n, 0)
                scatter(n, 1)

            @block.scalar
            def _(act):
                def silu(e, c):
                    ge(act, up_done, 6, e, c + 1)
                    ge(act, hid_turned, 6, e, c - 1)
                    act.activation(HID[:, c % 2, 0:CHUNKS[c][1]], PS[:, 2 * (c % 2), 0:CHUNKS[c][1]], ACT.Silu).then_inc(silu_done, 1)

                def turned(e, c):
                    n = CHUNKS[c][1] // P
                    ge(act, hid_turned, 6, e, c + 1)
                    if c == 0:
                        ge(act, down_done, 6, e, 0)
                    act.activation(HT[:, 4 * c:4 * c + n, :], PS[:, 4 + c % 2, 0:n * P].rearrange("p (i s) -> p i s", s=P),
                                   ACT.Copy).then_inc(ht_out, 1)

                def body(e, first, last):
                    silu(e, 0)
                    silu(e, 1)
                    for c in range(2, NC6):
                        turned(e, c - 2)
                        silu(e, c)
                    turned(e, NC6 - 2)
                    turned(e, NC6 - 1)
                    for half in range(2):
                        ge(act, down_done, 6, e, 3 * (half + 1))
                        ge(act, scattered, KT, e, 0)
                        act.activation(YE[:, half * 512:(half + 1) * 512], PS[:, 6 + half, :], ACT.Copy).then_inc(y_out, 1)
                loop(act, body)

            @block.vector
            def _(dve):
                chain = Chain(dve, chain_sem)
                evac = gated_residual(1, 1, tmp)
                LINKS = KT

                def select(e):
                    expert, chunk = expert_of(dve, e), chunk_of(dve, e)
                    ge(dve, gathered, 1, e, 0)
                    for t in range(3):
                        where = POS[:, t, expert:expert + 1] if isinstance(expert, int) else POS[:, t, bass.ds(expert, 1)]
                        last = dve.tensor_scalar(SL[:, t, :], one(IOTA, chunk), where, None, ALU.is_equal)
                    last.then_inc(sel_set, 1)

                def tokens(e):
                    ge(dve, gathered, 1, e, 1)
                    ge(dve, up_done, 6, e, 0)
                    for j in range(2):
                        dve.tensor_copy(XE[:, 4 * j:4 * j + 4, :], PS[:, j, :].rearrange("p (k s) -> p k s", s=P)).then_inc(xe_out, 1)

                def hidden(e, c):
                    ge(dve, silu_done, 6, e, c + 1)
                    width = CHUNKS[c][1]
                    dve.tensor_tensor(HID[:, c % 2, 0:width], HID[:, c % 2, 0:width], PS[:, 2 * (c % 2) + 1, 0:width], ALU.mult).then_inc(hid_done, 1)

                def add(e, part):
                    for k in range(4 * part, 4 * part + 4):
                        ge(dve, scattered, KT, e, k + 1 - KT)
                        if k:
                            ge(dve, added, KT, e, k - KT)
                        evac(dve, chain, k, PS[:, 4 + k % 4, 0:TOK], P).then_inc(added, 1)

                def body(e, first, last):
                    hidden(e, 0)
                    if not first:
                        add(e, 0)
                    hidden(e, 1)
                    if not first:
                        add(e, 1)
                    expert, chunk = expert_of(dve, e), chunk_of(dve, e)
                    slots = IOTAP[:, 0:1] if isinstance(chunk, int) else IOTAP[:, bass.ds(chunk, 1)]
                    ge(dve, scattered, KT, e, 0)
                    dve.scalar_tensor_tensor(GT[:], one(PB, expert), slots, one(GB, expert), ALU.is_equal, ALU.mult).then_inc(gt_set, 1)
                    if not last:
                        select(e + 1)
                    for c in range(2, NC6):
                        hidden(e, c)
                    if not last:
                        tokens(e + 1)

                dve.wait_ge(tables, 32)
                select(0)
                tokens(0)
                body(0, True, False)
                more = dve.value_load(ITEMS[0:1, 2 * (NE + MORE):2 * (NE + MORE) + 1], min_val=0, max_val=MORE)
                with dve.Fori(1, more + (NE - 1)) as e:
                    chain.enter(e - 1, LINKS)
                    body(e, False, False)
                    chain.leave(0)
                for e, tail in ((more + (NE - 1), False), (more + NE, True)):
                    chain.enter(e - 1, LINKS)
                    if tail:
                        add(e, 0)
                        add(e, 1)
                    else:
                        body(e, False, True)
                    chain.leave(0)

    phases = [0]

    def done():
        phases[0] += 1
        return stop is not None and phases[0] >= stop

    def phase(f, *args):
        with ExitStack() as own:
            stage.append(own)
            sems.clear()
            f(*args)
            nc.clear_and_free_semaphores(list(sems))
            nc.all_engine_barrier()
            stage.pop()
        return done()

    def run():
        if phase(setup_phase):
            return
        with ExitStack() as even:
            stage.append(even)
            QS, NATS = sb("QS", [P, 24, NS]), sb("NATS", [NS, 2048])
            with ExitStack() as prompt:
                stage.append(prompt)
                QKV, NAT = sb("QKV", [P, 24, TOK]), sb("NAT", [P, 3, 2048])
                if phase(norm_phase, 0) or phase(project_phase, io["w_in_even"], 0, 3 * 2 * W_MIX, 3, H, copy_to(QKV), True):
                    return
                if phase(kv_rows_phase, QKV, NAT) or phase(prompt_attention_phase, QKV, NAT):
                    return
                if phase(keep_samples_phase, QKV, NAT, QS, NATS):
                    return
                stage.pop()
            if phase(sample_attention_phase, QS, NATS):
                return
            stage.pop()
        if phase(residual_phase, io["w_out_even"], H, 0) or phase(norm_phase, 1) or phase(dense_phase):
            return
        if phase(norm_phase, 2):
            return
        with ExitStack() as odd:
            stage.append(odd)
            Y = sb("Y", [P, KT, TOK])
            with ExitStack() as d:
                stage.append(d)
                DD = sb("DD", [P, 16, TOK])
                if phase(project_phase, io["w_in_odd"], C_COLS, 4 * W_MIX, 3, H, copy_to(DD), True) or phase(retention_phase, DD, Y):
                    return
                stage.pop()
            AR, BK = sb("AR", [P, 4, NCH, 2, CH]), sb("BK", [P, 4, NCH, 2, CH])
            VS, PEND = sb("VS", [P, 4, NCH, CH]), sb("PEND", [P, 4, NCH])
            G, BON = sb("G_c", [P, 4, TOK]), sb("BON", [P, 4, TOK])
            with ExitStack() as c:
                stage.append(c)
                PC = sb("PC", [P, 15, TOK])
                if phase(clear_phase, PC[:, 14, :]) or phase(project_phase, io["w_in_odd"], 0, C_COLS, 3, H, copy_to(PC), True):
                    return
                if phase(rwkv_prepare_phase, PC, AR, BK, VS, G, BON, PEND):
                    return
                stage.pop()
            YT = sb("YT", [P, 4, TOK])
            if phase(rwkv_chunks_phase, AR, BK, VS, PEND, YT) or phase(rwkv_output_phase, YT, G, BON, Y):
                return
            if phase(residual_phase, io["w_out_odd"], Y, 1):
                return
            stage.pop()
        if phase(norm_phase, 3):
            return
        with ExitStack() as moe:
            stage.append(moe)
            GB, PB, ITEMS = sb("GB", [P, NE, TOK]), sb("PB", [P, NE, TOK]), sb("ITEMS", [1, 2 * (NE + MORE) + 1], I32)
            POS, HN = sb("POS", [P, 3, NE]), sb("HN", [P, 3, D])
            if phase(router_phase, GB, PB, POS, HN, ITEMS) or phase(experts_phase, GB, PB, POS, HN, ITEMS):
                return
            stage.pop()
        if phase(norm_phase, 4) or phase(store_phase):
            return

    with root:
        run()
    return nc


def shape_tables():
    f = np.float32
    log = lambda c: np.where(c > 0, np.log(np.maximum(c, 1)), NEG).astype(f)
    t = {"ident": np.eye(P, dtype=f)}

    def patterns(d):
        return ((d >= 0) & (d <= 128)).astype(int) + ((d >= 0) & (d % 4 == 0) & (d <= 512)) + ((d >= 0) & (d % 16 == 0) & (d <= 2048))

    q = np.arange(P)[:, None]
    k = np.arange(2 * P)[None, :]
    bias = np.zeros((P, 2, 384), f)
    for j, c, n in ((0, 0, P), (1, P, 2 * P)):
        d = q + j * P - k[:, :n]
        bias[:, 0, c:c + n] = log(patterns(d))
        bias[:, 1, c:c + n] = log((d >= 0).astype(int))
    t["prompt_bias"] = bias
    far = np.arange(FAR_TILES * P)
    rows = np.concatenate([16 * (far // 8) + far % 8, np.arange(FAR_TILES * 256, PAST)])
    row = np.arange(P)[:, None]
    tt, ss = row % DT, row // (2 * DT) % 2
    t["win_bias"] = log(patterns(PAST + tt - rows[None, :]))
    new = np.zeros((P, 2, NB // 2, NS), f)
    theirs, when = np.arange(NS) // DT, np.arange(NS) % DT
    d = tt - when[None, :]
    for pair in range(NB // 2):
        mine = theirs[None, :] == 2 * pair + ss
        new[:, 0, pair] = log(patterns(d) * mine)
        new[:, 1, pair] = log((d >= 0) * mine)
    t["new_bias"] = new
    t["head_mask"] = (np.arange(512)[None, :] // HD == row % 64 // DT).astype(f)
    t["token_select"] = (np.arange(2 * DT)[None, :] == DT * (row // 64) + row % DT).astype(f)
    i, j = np.arange(8)[:, None], np.arange(8)[None, :]
    t["tie"] = np.tile((j < i).astype(f).reshape(1, 64), (P, 1))
    angle = (1.0 / (f(10000.0) ** np.linspace(0.0, 1.0, HDD // 2, dtype=f))).astype(f)
    pos = np.concatenate([np.arange(SEQ), np.tile(PAST + np.arange(DT), NB)]).astype(f)
    theta = (np.repeat(angle, 2)[:, None] * pos[None, :]).astype(f)
    t["cos"], t["sin"] = np.cos(theta).astype(f), np.sin(theta).astype(f)
    rot = np.zeros((P, P), f)
    even = np.arange(0, P, 2)
    rot[even + 1, even], rot[even, even + 1] = -1, 1
    t["rotate"] = rot
    log_g = np.log1p(-(2.0 ** (-5.0 - np.arange(NHD))))
    size = np.concatenate([np.full(SEQ, 128), np.full(NS, DT)])
    at = np.concatenate([np.arange(SEQ) % 128, np.arange(NS) % DT])
    t["q_dec"] = np.tile(np.exp((at + 1.0)[None, :] * log_g[:, None]).astype(f)[None], (P, 1, 1))
    k_dec = np.zeros((3 * P, NHD), f)
    k_dec[:TOK] = np.exp((size - 1.0 - at)[:, None] * log_g[None, :]) * HDD ** -0.5
    t["k_dec"] = np.ascontiguousarray(k_dec.reshape(3, P, NHD).transpose(1, 0, 2))

    def decay(d):
        return np.where(d >= 0, np.exp(np.maximum(d, 0)[None] * log_g[:, None, None]), 0.0) * HDD ** -0.5

    d = np.arange(P)[None, :] - np.arange(P)[:, None]
    t["d_mask"] = np.ascontiguousarray(decay(d).transpose(1, 0, 2).astype(f))
    d = when[None, :] - when[:, None]
    t["d_mask_sample"] = np.ascontiguousarray((decay(d) * (theirs[None, :] == theirs[:, None])[None]).transpose(1, 0, 2).astype(f))
    t["sample_mask"] = (theirs[:, None] == np.arange(NB)[None, :]).astype(f)
    t["chunk_dec"] = np.tile(np.stack([np.exp(128 * log_g), np.exp(DT * log_g)]).astype(f)[None], (P, 1, 1))
    half = np.arange(P) // HD
    t["head_ones"] = (half[:, None] == half[None, :]).astype(f)
    starts = np.concatenate([np.arange(0, SEQ, CH), np.arange(SEQ, TOK, DT)])
    t["scan_reset"] = np.ones((P, TOK), f)
    t["scan_reset"][:, starts] = 0
    s_, q_ = np.arange(64)[:, None] % CH, np.arange(64)[None, :]
    t["chunk_mask"] = np.where(q_ < CH, s_ < q_, s_ <= q_ - CH).astype(f)
    t["before"] = np.triu(np.ones((P, P), f), 1)
    t["iota"] = np.tile(np.arange(3 * P, dtype=f).reshape(1, 3, P), (P, 1, 1))
    t["iota_p"] = np.arange(3 * P, dtype=f).reshape(3, P).T.copy()
    flag, order = np.meshgrid(np.arange(2 * NE), np.arange(MORE))
    t["item_table"] = np.stack([order, flag % NE, 1 + flag // NE]).astype(f)[None]
    t["expert_select"] = np.repeat(np.eye(NE, dtype=f)[:, :, None], P, axis=2)
    return t


_OUTS = [("y_prompt", (1, SEQ, D)), ("y_sample", (NB, DT, D)),
         ("win_prompt", (1, SEQ, 2, NH, HD)), ("win_sample", (NB, DT, 2, NH, HD)),
         ("moba_prompt", (1, SEQ, 2, NH, HD)), ("moba_sample", (NB, DT, 2, NH, HD)),
         ("rwkv_prompt", (1, NH, HD, HD)), ("rwkv_sample", (NB, NH, HD, HD)),
         ("shift_prompt", (1, C_COLS)), ("shift_sample", (NB, C_COLS)),
         ("ret_prompt", (1, NHD, HDD, HDD)), ("ret_sample", (NB, NHD, HDD, HDD))]
_VECTORS = [name for name, _ in VROWS]


def layout(inputs):
    rows = []
    for name, n in VROWS:
        v = np.asarray(inputs[name]).reshape(-1)
        rows.append(np.concatenate([v, np.zeros(n * P - v.size, v.dtype)]).reshape(n, P))
    arrays = {name: np.ascontiguousarray(a) for name, a in inputs.items() if name not in _VECTORS}
    arrays["vectors"] = np.concatenate(rows)
    arrays.update(shape_tables())
    return arrays


def build(nc, arrays, stop=None):
    io = {name: nc.dram_tensor(f"in_{name}", a.shape, mybir.dt.from_np(a.dtype), kind="ExternalInput").ap()
          for name, a in arrays.items()}
    for name, shape in _OUTS:
        io[name] = nc.dram_tensor(f"out_{name}", shape, F32, kind="ExternalOutput").ap()
    hybrid_step(nc, io, stop)


def kernel(**inputs):
    import concourse.bacc as bacc
    from concourse.bass_utils import run_bass_kernel_spmd

    nc = bacc.Bacc("TRN2", target_bir_lowering=False, num_devices=1)
    arrays = layout(inputs)
    build(nc, arrays)
    r = run_bass_kernel_spmd(nc, [{f"in_{name}": a for name, a in arrays.items()}], core_ids=[0])
    return tuple(r.results[0][f"out_{name}"] for name, _ in _OUTS)
```
